# Optimizing a Trainium2 kernel written in Bass

```python
import math
import jax, jax.numpy as jnp
from jax import lax
import numpy as np

D_MODEL = 2048
BATCH = 1
SEQ = 512
DEPTH = 1

N_MIXERS = 3
HEAD_DIM = 64
N_HEADS = D_MODEL // HEAD_DIM
N_KV = N_HEADS // 8
GQA_GROUP = N_HEADS // N_KV
Q_DIM = N_HEADS * HEAD_DIM
KV_DIM = N_KV * HEAD_DIM
ATTN_SCALE = HEAD_DIM ** -0.5
BLOCK = 128
SWA_WINDOW = 128
DIL_PATTERNS = ((128, 1), (512, 4), (2048, 16))
N_DIL = len(DIL_PATTERNS)
IDX_HEADS = 16
IDX_DIM = 64
TOPK_MAX = 256
D_FF = 256 * math.ceil(8 * D_MODEL / (3 * 256))
DEEPNORM_ALPHA = (2 * DEPTH) ** 0.25
DEEPNORM_BETA = (8 * DEPTH) ** -0.25
LN_EPS = 1e-5

A_IN = Q_DIM + 2 * KV_DIM
B_IN = N_DIL * (Q_DIM + 2 * KV_DIM)
C_SPLITS = (Q_DIM, Q_DIM + KV_DIM, Q_DIM + 2 * KV_DIM,
            Q_DIM + 2 * KV_DIM + IDX_HEADS * IDX_DIM,
            Q_DIM + 2 * KV_DIM + IDX_HEADS * IDX_DIM + IDX_DIM)
C_IN = C_SPLITS[-1] + IDX_HEADS

kernel_name = 'hybrid_swa_dilated_dsa_deepnorm'

def _n_layers_of(kind):
    return len(range(kind, DEPTH, N_MIXERS))

def alibi_slopes(n):
    return jnp.asarray(2.0 ** (-8.0 * np.arange(1, n + 1) / n), dtype=jnp.float32)

def layer_norm(x, g, b):
    xf = x.astype(jnp.float32)
    mu = xf.mean(-1, keepdims=True)
    var = jnp.square(xf - mu).mean(-1, keepdims=True)
    return ((xf - mu) * lax.rsqrt(var + LN_EPS) * g + b).astype(x.dtype)

def swiglu_ffn(x, w_gate_up, w_down):
    g, u = jnp.split(x @ w_gate_up, 2, axis=-1)
    return (jax.nn.silu(g) * u) @ w_down

def swa_sink_attention(x, w_in, sinks, w_out):
    B, S, _ = x.shape
    nb = S // BLOCK
    q, k, v = jnp.split(x @ w_in, [Q_DIM, Q_DIM + KV_DIM], axis=-1)
    q = q.reshape(B, nb, BLOCK, N_KV, GQA_GROUP, HEAD_DIM)
    k = k.reshape(B, nb, BLOCK, N_KV, HEAD_DIM)
    v = v.reshape(B, nb, BLOCK, N_KV, HEAD_DIM)

    def with_prev(t):
        prev = jnp.concatenate([jnp.zeros_like(t[:, :1]), t[:, :-1]], axis=1)
        return jnp.concatenate([prev, t], axis=2)

    kb, vb = with_prev(k), with_prev(v)
    s = jnp.einsum('bnqkgd,bnskd->bnkgqs', q, kb).astype(jnp.float32) * ATTN_SCALE
    qpos = jnp.arange(BLOCK)[:, None] + BLOCK
    kpos = jnp.arange(2 * BLOCK)[None, :]
    dist = qpos - kpos
    in_window = (dist >= 0) & (dist < SWA_WINDOW)
    has_prev = (jnp.arange(nb) > 0)[:, None, None] | (kpos >= BLOCK)[None]
    valid = in_window[None] & has_prev
    slopes = alibi_slopes(N_HEADS).reshape(N_KV, GQA_GROUP)[:, :, None, None]
    s = jnp.where(valid[None, :, None, None], s - slopes * dist, -jnp.inf)
    sink = sinks.astype(jnp.float32).reshape(N_KV, GQA_GROUP)[:, :, None, None]
    m = jnp.maximum(s.max(-1, keepdims=True), sink)
    p = jnp.exp(s - m)
    p = p / (p.sum(-1, keepdims=True) + jnp.exp(sink - m))
    o = jnp.einsum('bnkgqs,bnskd->bnqkgd', p.astype(vb.dtype), vb)
    return o.reshape(B, S, Q_DIM) @ w_out

def dilated_attention(x, w_in, w_out):
    B, S, _ = x.shape
    nb = S // BLOCK
    h = (x @ w_in).reshape(B, S, N_DIL, Q_DIM + 2 * KV_DIM)
    q = h[..., :Q_DIM].reshape(B, S, N_DIL, N_KV, GQA_GROUP, HEAD_DIM)
    k = h[..., Q_DIM:Q_DIM + KV_DIM].reshape(B, S, N_DIL, N_KV, HEAD_DIM)
    v = h[..., Q_DIM + KV_DIM:].reshape(B, S, N_DIL, N_KV, HEAD_DIM)
    k_groups = [k[:, :, g] for g in range(N_DIL)]
    v_groups = [v[:, :, g] for g in range(N_DIL)]
    slopes = alibi_slopes(N_HEADS).reshape(N_KV, GQA_GROUP)[:, :, None, None]

    def block(i):
        t = i * BLOCK + jnp.arange(BLOCK)
        qb = lax.dynamic_slice_in_dim(q, i * BLOCK, BLOCK, axis=1)
        outs, lses = [], []
        for g, (window, dilation) in enumerate(DIL_PATTERNS):
            dist = jnp.arange(window // dilation + 1) * dilation
            pos = t[:, None] - dist[None, :]
            valid = pos >= 0
            pos = jnp.maximum(pos, 0)
            kg = k_groups[g][:, pos]
            vg = v_groups[g][:, pos]
            s = jnp.einsum('bqkgd,bqjkd->bkgqj', qb[:, :, g], kg).astype(jnp.float32) * ATTN_SCALE
            s = jnp.where(valid, s - slopes * dist, -jnp.inf)
            lse = jax.nn.logsumexp(s, axis=-1)
            p = jnp.exp(s - lse[..., None])
            outs.append(jnp.einsum('bkgqj,bqjkd->bqkgd', p.astype(vg.dtype), vg))
            lses.append(lse.transpose(0, 3, 1, 2))
        wts = jax.nn.softmax(jnp.stack(lses), axis=0)
        o = jnp.sum(wts[..., None] * jnp.stack(outs).astype(jnp.float32), axis=0)
        return o.reshape(B, BLOCK, Q_DIM).astype(x.dtype)

    o = lax.map(block, jnp.arange(nb))
    o = jnp.moveaxis(o, 0, 1).reshape(B, S, Q_DIM)
    return o @ w_out

def dsa_sparse_attention(x, w_in, w_out):
    B, S, _ = x.shape
    nb = S // BLOCK
    top_k = min(TOPK_MAX, S // 4)
    q, k, v, qi, ki, wi = jnp.split(x @ w_in, list(C_SPLITS), axis=-1)
    q = q.reshape(B, S, N_KV, GQA_GROUP, HEAD_DIM)
    k = k.reshape(B, S, N_KV, HEAD_DIM)
    v = v.reshape(B, S, N_KV, HEAD_DIM)
    qi = qi.reshape(B, S, IDX_HEADS, IDX_DIM)
    wi = wi.astype(jnp.float32) * IDX_HEADS ** -0.5
    kpos = jnp.arange(S)
    slopes = alibi_slopes(N_HEADS).reshape(N_KV, GQA_GROUP)[None, :, :, None, None]
    gather = jax.vmap(lambda tab, idx: tab[idx])

    def block(i):
        t = i * BLOCK + jnp.arange(BLOCK)
        qib = lax.dynamic_slice_in_dim(qi, i * BLOCK, BLOCK, axis=1)
        wib = lax.dynamic_slice_in_dim(wi, i * BLOCK, BLOCK, axis=1)
        rel = jax.nn.relu(jnp.einsum('bqhd,bsd->bqhs', qib, ki).astype(jnp.float32) * IDX_DIM ** -0.5)
        score = jnp.einsum('bqhs,bqh->bqs', rel, wib)
        score = jnp.where(kpos[None, None, :] <= t[None, :, None], score, -jnp.inf)
        _, idx = lax.top_k(score, top_k)
        valid = idx <= t[None, :, None]
        kg = gather(k, idx)
        vg = gather(v, idx)
        qb = lax.dynamic_slice_in_dim(q, i * BLOCK, BLOCK, axis=1)
        s = jnp.einsum('bqkgd,bqjkd->bkgqj', qb, kg).astype(jnp.float32) * ATTN_SCALE
        dist = (t[None, :, None] - idx)[:, None, None]
        s = jnp.where(valid[:, None, None], s - slopes * dist, -jnp.inf)
        p = jax.nn.softmax(s, axis=-1)
        o = jnp.einsum('bkgqj,bqjkd->bqkgd', p.astype(vg.dtype), vg)
        return o.reshape(B, BLOCK, Q_DIM)

    o = lax.map(block, jnp.arange(nb))
    o = jnp.moveaxis(o, 0, 1).reshape(B, S, Q_DIM)
    return o @ w_out

def setup_inputs(seed: int = 0) -> dict:
    key = jax.random.key(seed)
    ks = jax.random.split(key, 12)
    n_a, n_b, n_c = (_n_layers_of(m) for m in range(N_MIXERS))

    def nrm(k, shape, scale):
        return jax.random.normal(k, shape, jnp.float32) * scale

    out_scale = Q_DIM ** -0.5 * DEEPNORM_BETA
    return {
        'x': nrm(ks[0], (BATCH, SEQ, D_MODEL), 1.0),
        'a_w_in': nrm(ks[1], (n_a, D_MODEL, A_IN), D_MODEL ** -0.5),
        'a_sinks': nrm(ks[2], (n_a, N_HEADS), 0.5),
        'a_w_out': nrm(ks[3], (n_a, Q_DIM, D_MODEL), out_scale),
        'b_w_in': nrm(ks[4], (n_b, D_MODEL, B_IN), D_MODEL ** -0.5),
        'b_w_out': nrm(ks[5], (n_b, Q_DIM, D_MODEL), out_scale),
        'c_w_in': nrm(ks[6], (n_c, D_MODEL, C_IN), D_MODEL ** -0.5),
        'c_w_out': nrm(ks[7], (n_c, Q_DIM, D_MODEL), out_scale),
        'ln_g': 1.0 + nrm(ks[8], (DEPTH, 2, D_MODEL), 0.02),
        'ln_b': nrm(ks[9], (DEPTH, 2, D_MODEL), 0.02),
        'ffn_w_gate_up': nrm(ks[10], (DEPTH, D_MODEL, 2 * D_FF), D_MODEL ** -0.5),
        'ffn_w_down': nrm(ks[11], (DEPTH, D_FF, D_MODEL), D_FF ** -0.5 * DEEPNORM_BETA),
    }

def reference(x, a_w_in, a_sinks, a_w_out, b_w_in, b_w_out, c_w_in, c_w_out, ln_g, ln_b, ffn_w_gate_up, ffn_w_down):
    for i in range(DEPTH):
        kind, j = i % N_MIXERS, i // N_MIXERS
        if kind == 0:
            y = swa_sink_attention(x, a_w_in[j], a_sinks[j], a_w_out[j])
        elif kind == 1:
            y = dilated_attention(x, b_w_in[j], b_w_out[j])
        else:
            y = dsa_sparse_attention(x, c_w_in[j], c_w_out[j])
        x = layer_norm(DEEPNORM_ALPHA * x + y, ln_g[i, 0], ln_b[i, 0])
        x = layer_norm(DEEPNORM_ALPHA * x + swiglu_ffn(x, ffn_w_gate_up[i], ffn_w_down[i]), ln_g[i, 1], ln_b[i, 1])
    return x


_drawn_inputs = setup_inputs


def setup_inputs(seed=0):
    import zlib

    import numpy as np

    out = dict(_drawn_inputs(seed))
    spreads = {}
    factors = {'a_sinks': 3.987}
    for name, (base, spread) in spreads.items():
        noise = np.random.default_rng([zlib.crc32(name.encode()), seed]).standard_normal(out[name].shape)
        drawn = base * np.exp(spread * noise) if base else spread * noise
        out[name] = __import__('jax').numpy.asarray(drawn.astype(out[name].dtype))
    for name, factor in factors.items():
        out[name] = (out[name] * factor).astype(out[name].dtype)
    return out
```

```python
from contextlib import ExitStack

import concourse.bass as bass
from concourse import mybir

F32 = mybir.dt.float32
F32R = mybir.dt.float32r
I32 = mybir.dt.int32
ALU = mybir.AluOpType
ACT = mybir.ActivationFunctionType

P = 128
LN_EPS = 1e-5
DEPTH = 1
ALPHA = (2 * DEPTH) ** 0.25
HEAD_DIM = 64
N_HEADS = 32
GQA = 8
WINDOW = 128
MASKED = 1.0e30


def trunk_layer(nc, x, w_in, sinks, w_out, ln_g, ln_b, w_gu, w_dn, out):
    S, D = x.shape[1], x.shape[2]
    Q_DIM = N_HEADS * HEAD_DIM
    KV_DIM = (w_in.shape[2] - Q_DIM) // 2
    FF = w_dn.shape[1]
    TT = S // P
    KD = D // P
    NN = D // 512
    KVH = N_HEADS // GQA
    TPJ = GQA // 2
    GC = 4
    NG = FF // P // GC
    HS = 1024
    A_UNITS = TPJ + 1 + NN
    B_UNITS = 2 * GC + NN
    assert S == 512 and D == 2048 and FF % (P * GC) == 0 and A_UNITS == 9 and B_UNITS == 12
    SCALE = HEAD_DIM ** -0.5
    SLOPE = [2.0 ** (-8.0 * (r + 1) / N_HEADS) for r in range(GQA)]
    SLOPE_STEP = 2.0 ** (-8.0 * GQA / N_HEADS)

    x_rows = x.rearrange("o (t p) d -> (o p) t d", p=P)
    out_rows = out.rearrange("o (t p) d -> (o p) t d", p=P)
    win_v = w_in.rearrange("o (k p) m -> (o p) k m", p=P)
    wout_v = w_out.rearrange("o (k p) m -> (o p) k m", p=P)
    wgu_v = w_gu.rearrange("o (k p) m -> (o p) k m", p=P)
    wdn_v = w_dn.rearrange("o (k p) m -> (o p) k m", p=P)

    with ExitStack() as ctx:
        def sb(name, shape, dt=F32):
            return ctx.enter_context(nc.sbuf_tensor(name, shape, dt))

        def sem(name):
            return ctx.enter_context(nc.semaphore(name))

        xt_hi = sb("xt_hi", [P, KD, S], F32R)
        xt_lo = sb("xt_lo", [P, KD, S], F32R)
        acc = sb("acc", [P, TT, D])
        raw = sb("raw", [P, 3, 2 * HS])
        w_hi = sb("w_hi", [P, 3, HS], F32R)
        w_lo = sb("w_lo", [P, 3, HS], F32R)
        ht_hi = sb("ht_hi", [P, 4, S], F32R)
        ht_lo = sb("ht_lo", [P, 4, S], F32R)
        ident = sb("ident", [P, P])
        eps = sb("eps", [P, 1])
        stats = sb("stats", [P, TT, NN * 6])
        meanvar = sb("meanvar", [P, TT, 2])
        std = sb("std", [P, TT])
        rstd = sb("rstd", [P, TT])

        with ExitStack() as a_ctx:
            def sa(name, shape, dt=F32):
                return a_ctx.enter_context(nc.sbuf_tensor(name, shape, dt))

            k_hi = sa("k_hi", [P, S], F32R)
            k_lo = sa("k_lo", [P, S], F32R)
            v_hi = sa("v_hi", [P, TT, 192], F32R)
            v_lo = sa("v_lo", [P, TT, 192], F32R)
            vt = sa("vt", [HEAD_DIM, S])
            q_st = sa("q_st", [P, 2, S], F32R)
            bias = sa("bias", [P, 2, 2, 256])
            prob = sa("prob", [P, 2, 2, 896])
            pt_hi = sa("pt_hi", [P, 2, 512], F32R)
            pt_lo = sa("pt_lo", [P, 2, 512], F32R)
            dist = sa("dist", [P, 256])
            dist_i = sa("dist_i", [P, 256], I32)
            sink_all = sa("sink_all", [P, N_HEADS])
            sink_j = sa("sink_j", [P, GQA])
            rmax = sa("rmax", [P, 2, 2, TT])
            negm = sa("negm", [P, 2, 2, TT])
            esink = sa("esink", [P, 2, 2, TT])
            rsum = sa("rsum", [P, 2, 2, TT])
            den = sa("den", [P, 2, 2, TT])
            rden = sa("rden", [P, 2, 2, TT])
        with ExitStack() as b_ctx:
            def sb2(name, shape, dt=F32):
                return b_ctx.enter_context(nc.sbuf_tensor(name, shape, dt))

            lng = sb2("lng", [P, D])
            lnb = sb2("lnb", [P, D])
            sg = sb2("sg", [P, S])
            hm = sb2("hm", [P, S])

        ps = ctx.enter_context(nc.psum_tensor("ps", [P, 8, 512], F32))
        SCORE_BANK = (4, 5)
        PT_BANK, PV_BANK = 6, 7
        A_BANKS = ([1, 2, 3, 0], [4, 5, 7, 6])
        A_BANKS_LAST = ([0, 1, 2, 3], [4, 5, 7, 6])
        B_BANKS = ([0, 1, 2, 3], [4, 5, 6, 7])

        x_in = [sem(f"x_in{t}") for t in range(TT)]
        raw_in = [sem(f"raw_in{s}") for s in range(3)]
        rawv_in = sem("rawv_in")
        sinks_in = sem("sinks_in")
        ln1_in = sem("ln1_in")
        ln2_in = sem("ln2_in")
        out_sent = sem("out_sent")
        consts = sem("consts")
        hi_made = sem("hi_made")
        lo_made = sem("lo_made")
        w_used = sem("w_used")
        xt_tr = sem("xt_tr")
        xt_hi_made = sem("xt_hi_made")
        xt_lo_made = sem("xt_lo_made")
        q_hi_made = sem("q_hi_made")
        q_lo_made = sem("q_lo_made")
        kv_hi_made = sem("kv_hi_made")
        k_lo_made = sem("k_lo_made")
        v_tr = sem("v_tr")
        v_hi_made = sem("v_hi_made")
        v_lo_made = sem("v_lo_made")
        sink_set = sem("sink_set")
        bias_set = sem("bias_set")
        dist_set = sem("dist_set")
        s_done = sem("s_done")
        s_read = sem("s_read")
        negm_made = sem("negm_made")
        exp_made = sem("exp_made")
        den_made = sem("den_made")
        rden_made = sem("rden_made")
        p_made = sem("p_made")
        pt_tr = sem("pt_tr")
        pt_hi_made = sem("pt_hi_made")
        pt_lo_made = sem("pt_lo_made")
        pv_done = sem("pv_done")
        o_hi_made = sem("o_hi_made")
        o_lo_made = sem("o_lo_made")
        a_sum = sem("a_sum")
        a_added = sem("a_added")
        b_sum = sem("b_sum")
        b_added = sem("b_added")
        stat_made = sem("stat_made")
        mean_made = sem("mean_made")
        std_made = sem("std_made")
        rstd_made = sem("rstd_made")
        centered = sem("centered")
        ln_made = sem("ln_made")
        sg_made = sem("sg_made")
        hm_made = sem("hm_made")
        h_hi_made = sem("h_hi_made")
        h_lo_made = sem("h_lo_made")

        waited_dve = sem("waited_dve")
        waited_pool = sem("waited_pool")
        waited_pe = sem("waited_pe")

        block = ctx.enter_context(nc.Block())

        def halves(third, off):
            return 6 * third + 2 * off

        def half_slot(off, h):
            return (2 * off + h) % 3

        def block_cols(b):
            return max(256 * b - 128, 0), 256 * b

        @block.sync
        def _(sp):
            def load(third, off, src, wait=True):
                if wait:
                    sp.wait_ge(lo_made, halves(third, off) - 4)
                n = src.shape[2]
                dst = raw[:, off % 3, :].rearrange("p (k n) -> p k n", n=n)
                sp.dma_start(dst, src).then_inc(raw_in[off % 3], 16)

            def load_q(third, off, j, i):
                load(third, off, win_v[:, :, bass.ds(512 * j + P * i, P)], wait=not first_units(third, off))

            def first_units(third, off):
                return isinstance(third, int) and 3 * third + off < 3

            def load_kv(third, off, j):
                if not first_units(third, off):
                    sp.wait_ge(lo_made, halves(third, off) - 4)
                dst = raw[:, off % 3, :].rearrange("p (k n) -> p k n", n=P)
                sp.dma_start(dst[:, :, 0:64], win_v[:, :, bass.ds(Q_DIM + 64 * j, 64)]).then_inc(raw_in[off % 3], 16)
                sp.dma_start(dst[:, :, 64:128], win_v[:, :, bass.ds(Q_DIM + KV_DIM + 64 * j, 64)])\
                  .then_inc(rawv_in, 16)

            def load_wout(third, off, j, n):
                load(third, off, wout_v[:, bass.ds(4 * j, 4), n * 512:(n + 1) * 512])

            for t in range(2):
                sp.dma_start(acc[:, t, :], x_rows[:, t, :]).then_inc(x_in[t], 16)
            load_kv(0, 0, 0)
            for t in range(2, TT):
                sp.dma_start(acc[:, t, :], x_rows[:, t, :]).then_inc(x_in[t], 16)
            load_q(0, 1, 0, 0)
            load_q(0, 2, 0, 1)
            with sp.Fori(0, KVH - 1) as j:
                third = 3 * j
                load_q(third, 3, j, 2)
                load_q(third, 4, j, 3)
                load_kv(third, 5, j + 1)
                for n in range(NN):
                    load_wout(third, 6 + n, j, n)
                load_q(third, 10, j, 4)
                load_q(third, 11, j, 5)
            j, third = KVH - 1, 3 * (KVH - 1)
            load_q(third, 3, j, 2)
            load_q(third, 4, j, 3)
            for n in range(NN):
                load_wout(third, 5 + n, j, n)
            sp.wait_ge(o_lo_made, TPJ * KVH)
            sp.dma_start(lng[:, :], ln_g[0, 0, :].partition_broadcast(P)).then_inc(ln1_in, 16)
            sp.dma_start(lnb[:, :], ln_b[0, 0, :].partition_broadcast(P)).then_inc(ln1_in, 16)
            with sp.Fori(0, NG) as g:
                third = 4 * g + 12
                for c in range(GC):
                    load(third, 2 * c, wgu_v[:, :, bass.ds(512 * g + P * c, P)])
                    load(third, 2 * c + 1, wgu_v[:, :, bass.ds(FF + 512 * g + P * c, P)])
                for n in range(NN):
                    load(third, 2 * GC + n, wdn_v[:, bass.ds(4 * g, 4), n * 512:(n + 1) * 512])
            sp.wait_ge(ln_made, TT)
            sp.dma_start(lng[:, :], ln_g[0, 1, :].partition_broadcast(P)).then_inc(ln2_in, 16)
            sp.dma_start(lnb[:, :], ln_b[0, 1, :].partition_broadcast(P)).then_inc(ln2_in, 16)
            for t in range(TT):
                sp.wait_ge(ln_made, TT + t + 1)
                sp.dma_start(out_rows[:, t, :], acc[:, t, :]).then_inc(out_sent, 16)
            sp.wait_ge(out_sent, 16 * TT)

        @block.gpsimd
        def _(pool):
            nc.gpsimd.memset(ident[:, :], 0.0).then_inc(consts, 1)
            pool.wait_ge(consts, 1)
            nc.gpsimd.affine_select(out=ident[:, :], in_=ident[:, :], compare_op=ALU.not_equal, fill=1.0,
                                    base=0, pattern=[[-1, P]], channel_multiplier=1).then_inc(consts, 1)
            nc.gpsimd.memset(eps[:, :], LN_EPS).then_inc(consts, 1)
            nc.gpsimd.memset(v_hi[:, :, :].bitcast(F32), 0.0).then_inc(consts, 1)
            nc.gpsimd.memset(v_lo[:, :, :].bitcast(F32), 0.0).then_inc(consts, 1)
            nc.gpsimd.iota(dist_i[:, :], pattern=[[-1, 256]], base=P, channel_multiplier=1).then_inc(consts, 1)
            pool.wait_ge(consts, 6)
            nc.gpsimd.tensor_copy(dist[:, :], dist_i[:, :]).then_inc(consts, 1)
            pool.wait_ge(consts, 7)
            nc.gpsimd.affine_select(out=dist[:, :], in_=dist[:, :], compare_op=ALU.is_ge, fill=MASKED,
                                    base=P, pattern=[[-1, 256]], channel_multiplier=1).then_inc(consts, 1)
            pool.wait_ge(consts, 8)
            nc.gpsimd.affine_select(out=dist[:, :], in_=dist[:, :], compare_op=ALU.is_ge, fill=MASKED,
                                    base=WINDOW - 1 - P, pattern=[[1, 256]], channel_multiplier=-1).then_inc(consts, 1)
            pool.wait_ge(consts, 9)
            pool.wait_ge(sinks_in, 16)

            def kv_head(j, last):
                pool.wait_ge(a_added, 16 * j + 1)
                pool.sem_inc(waited_pool, 1)
                nc.gpsimd.tensor_copy(sink_j[:, :], sink_all[:, bass.ds(GQA * j, GQA)]).then_inc(sink_set, 1)
                for i in range(TPJ):
                    if i >= 2:
                        pool.wait_ge(s_read, 16 * j + 4 * (i - 1))
                    pool.sem_inc(waited_pool, 1)
                    for h in range(2):
                        step = nc.gpsimd.tensor_scalar(bias[:, i % 2, h, :], dist[:, :], -SLOPE[2 * i + h], None, ALU.mult)
                    step.then_inc(bias_set, 1)
                if not last:
                    pool.wait_ge(bias_set, TPJ * j + TPJ)
                    pool.sem_inc(waited_pool, 1)
                    nc.gpsimd.tensor_scalar(dist[:, :], dist[:, :], SLOPE_STEP, None, ALU.mult).then_inc(dist_set, 1)
                    pool.wait_ge(dist_set, j + 1)

            def scale_residual(phase, added):
                for t in range(TT):
                    pool.wait_ge(xt_tr, 16 * phase + 4 * t + 4)
                    nc.gpsimd.tensor_scalar(acc[:, t, :], acc[:, t, :], ALPHA, None, ALU.mult).then_inc(added, 1)

            scale_residual(0, a_added)
            with pool.Fori(0, KVH - 1) as j:
                kv_head(j, False)
            kv_head(KVH - 1, True)
            scale_residual(1, b_added)

        @block.scalar
        def _(act):
            def split_hi(third, off, h, first=False, kv=None):
                if h == 0:
                    act.wait_ge(raw_in[off % 3], 16 * (third + off // 3 + 1))
                    if kv is not None:
                        act.wait_ge(rawv_in, 16 * (kv + 1))
                if not first:
                    act.wait_ge(w_used, halves(third, off) + h - 2)
                nc.scalar.activation(w_hi[:, half_slot(off, h), :], raw[:, off % 3, h * HS:(h + 1) * HS],
                                     ACT.Copy).then_inc(hi_made, 1)

            def xt_evac(phase):
                for e in range(16):
                    t, q = divmod(e, 4)
                    act.wait_ge(xt_tr, 16 * phase + e + 1)
                    nc.scalar.activation(xt_hi[:, 4 * q:4 * q + 4, t * P:(t + 1) * P],
                                         ps[:, e % 8, :].rearrange("p (k n) -> p k n", n=P),
                                         ACT.Copy).then_inc(xt_hi_made, 1)

            def kv_evac(third, off, m):
                act.wait_ge(w_used, halves(third, off) + 2)
                nc.scalar.activation(k_hi[0:64, :], ps[0:64, 0, :], ACT.Copy)
                nc.scalar.activation(k_hi[64:128, :], ps[0:64, 0, :], ACT.Copy)
                nc.scalar.activation(vt[:, :], ps[64:128, 0, :], ACT.Copy).then_inc(kv_hi_made, 1)

            def v_evac(m):
                act.wait_ge(v_tr, m + 1)
                nc.scalar.activation(v_hi[:, :, 64:128], ps[:, PT_BANK, 0:256].rearrange("p (c d) -> p c d", d=64),
                                     ACT.Copy).then_inc(v_hi_made, 1)

            def q_evac(third, off, i):
                act.wait_ge(w_used, halves(third, off) + 2)
                nc.scalar.activation(q_st[0:64, 0, :], ps[0:64, i, :], ACT.Copy, scale=SCALE).then_inc(q_hi_made, 1)
                nc.scalar.activation(q_st[64:128, 1, :], ps[64:128, i, :], ACT.Copy, scale=SCALE).then_inc(q_hi_made, 1)

            def exps(a, i, h):
                act.wait_ge(negm_made, 2 * a + h + 1)
                nc.scalar.activation(esink[:, i % 2, h, :], negm[:, i % 2, h, :], ACT.Exp,
                                     bias=sink_j[:, 2 * i + h:2 * i + h + 1])
                for b in range(TT):
                    c0, own = block_cols(b)
                    c1 = own + 128
                    step = nc.scalar.activation(prob[:, i % 2, h, c0:c1], prob[:, i % 2, h, c0:c1], ACT.Exp,
                                                bias=negm[:, i % 2, h, b:b + 1],
                                                accum_out=rsum[:, i % 2, h, b:b + 1])
                step.then_inc(exp_made, 1)

            def pt_evac(b, y):
                n = 384 if y % 2 else 512
                if y >= 2:
                    act.wait_ge(pv_done, 4 * b + y - 1)
                act.wait_ge(pt_tr, 4 * b + y + 1)
                nc.scalar.activation(pt_hi[:, y % 2, 0:n], ps[:, PT_BANK, 0:n], ACT.Copy).then_inc(pt_hi_made, 1)

            def o_evac(b, i):
                act.wait_ge(pv_done, 4 * b + 4)
                nc.scalar.activation(ht_hi[:, i, :], ps[:, PV_BANK, :], ACT.Copy).then_inc(o_hi_made, 1)

            def attention(j, third, last):
                a = 4 * j
                split_hi(third, 2, 0)
                split_hi(third, 2, 1)
                for i in range(1, 4 if last else 5):
                    kv = j + 1 if (i == 3 and not last) else None
                    q_evac(third, i, i - 1)
                    if i >= 3:
                        o_evac(a + i - 3, i - 3)
                    split_hi(third, i + 2, 0, kv=kv)
                    if i >= 2:
                        pt_evac(a + i - 2, 0)
                    exps(a + i - 1, i - 1, 0)
                    if i >= 2:
                        pt_evac(a + i - 2, 1)
                    split_hi(third, i + 2, 1)
                    if i >= 2:
                        pt_evac(a + i - 2, 2)
                    exps(a + i - 1, i - 1, 1)
                    if i >= 2:
                        pt_evac(a + i - 2, 3)
                if last:
                    q_evac(third, 4, 3)
                    o_evac(a + 1, 1)
                    split_hi(third, 6, 0)
                    pt_evac(a + 2, 0)
                    exps(a + 3, 3, 0)
                    for y in (1, 2, 3):
                        pt_evac(a + 2, y)
                    o_evac(a + 2, 2)
                    exps(a + 3, 3, 1)
                    split_hi(third, 6, 1)
                    for y in range(4):
                        pt_evac(a + 3, y)
                    o_evac(a + 3, 3)
                else:
                    kv_evac(third, 5, j + 1)
                    o_evac(a + 2, 2)
                    pt_evac(a + 3, 0)
                    split_hi(third, 7, 0)
                    pt_evac(a + 3, 1)
                    pt_evac(a + 3, 2)
                    split_hi(third, 7, 1)
                    pt_evac(a + 3, 3)
                    o_evac(a + 3, 3)
                    v_evac(j + 1)
                first_row = 5 if last else 6
                for n in range(1, NN):
                    for h in range(2):
                        split_hi(third, first_row + n + 1, h)

            def layer_norm_std(which):
                for t in range(TT):
                    act.wait_ge(mean_made, TT * which + t + 1)
                    nc.scalar.activation(std[:, t:t + 1], meanvar[:, t, 1:2], ACT.Sqrt,
                                         bias=eps[:, :]).then_inc(std_made, 1)

            def ffn_group(g, third, last):
                for c in range(GC):
                    for h in range(2):
                        split_hi(third, 2 * c + 1, h)
                    act.wait_ge(w_used, halves(third, 2 * c) + 2)
                    nc.scalar.activation(sg[:, :], ps[:, 2 * c, :], ACT.Silu).then_inc(sg_made, 1)
                    for h in range(2):
                        split_hi(third, 2 * c + 2, h)
                    act.wait_ge(hm_made, 4 * g + c + 1)
                    nc.scalar.activation(ht_hi[:, c, :], hm[:, :], ACT.Copy).then_inc(h_hi_made, 1)
                for n in range(NN - 1 if last else NN):
                    for h in range(2):
                        split_hi(third, 2 * GC + n + 1, h)

            act.dma_start(sink_all[:, :], sinks[0, :].partition_broadcast(P)).then_inc(sinks_in, 16)
            xt_evac(0)
            split_hi(0, 0, 0, first=True, kv=0)
            split_hi(0, 0, 1, first=True)
            split_hi(0, 1, 0, first=True)
            split_hi(0, 1, 1)
            kv_evac(0, 0, 0)
            act.wait_ge(consts, 5)
            v_evac(0)
            with act.Fori(0, KVH - 1) as j:
                attention(j, 3 * j, False)
            attention(KVH - 1, 3 * (KVH - 1), True)
            layer_norm_std(0)
            xt_evac(1)
            with act.Fori(0, NG - 1) as g:
                ffn_group(g, 4 * g + 12, False)
            ffn_group(NG - 1, 4 * (NG - 1) + 12, True)
            layer_norm_std(1)

        @block.vector
        def _(dve):
            def split_lo(third, off, h):
                dve.wait_ge(hi_made, halves(third, off) + h + 1)
                nc.vector.tensor_tensor(w_lo[:, half_slot(off, h), :], raw[:, off % 3, h * HS:(h + 1) * HS],
                                        w_hi[:, half_slot(off, h), :].bitcast(F32), ALU.subtract).then_inc(lo_made, 1)

            def xt_evac(phase):
                for e in range(16):
                    t, q = divmod(e, 4)
                    dve.wait_ge(xt_hi_made, 16 * phase + e + 1)
                    nc.vector.tensor_tensor(xt_lo[:, 4 * q:4 * q + 4, t * P:(t + 1) * P],
                                            ps[:, e % 8, :].rearrange("p (k n) -> p k n", n=P),
                                            xt_hi[:, 4 * q:4 * q + 4, t * P:(t + 1) * P].bitcast(F32),
                                            ALU.subtract).then_inc(xt_lo_made, 1)

            def kv_evac(m):
                dve.wait_ge(kv_hi_made, m + 1)
                nc.vector.tensor_tensor(k_lo[0:64, :], ps[0:64, 0, :], k_hi[0:64, :].bitcast(F32), ALU.subtract)
                nc.vector.tensor_tensor(k_lo[64:128, :], ps[0:64, 0, :], k_hi[0:64, :].bitcast(F32),
                                        ALU.subtract).then_inc(k_lo_made, 1)

            def v_evac(m):
                dve.wait_ge(v_hi_made, m + 1)
                nc.vector.tensor_tensor(v_lo[:, :, 64:128], ps[:, PT_BANK, 0:256].rearrange("p (c d) -> p c d", d=64),
                                        v_hi[:, :, 64:128].bitcast(F32), ALU.subtract).then_inc(v_lo_made, 1)

            def q_evac(a, i):
                for h in range(2):
                    top = slice(64 * h, 64 * h + 64)
                    other = slice(64 - 64 * h, 128 - 64 * h)
                    dve.wait_ge(q_hi_made, 2 * a + h + 1)
                    nc.vector.scalar_tensor_tensor(out=q_st[other, h, :], in0=ps[top, i, :], scalar=SCALE,
                                                   in1=q_st[top, h, :].bitcast(F32), op0=ALU.mult,
                                                   op1=ALU.subtract).then_inc(q_lo_made, 1)

            def scores(a, i, group):
                h, half = divmod(group, 2)
                if group == 0:
                    dve.wait_ge(bias_set, a + 1)
                dve.wait_ge(s_done, 4 * a + group + 1)
                dve.sem_inc(waited_dve, 1)
                at = 0
                for b in (2 * half, 2 * half + 1):
                    n = 128 if b == 0 else 256
                    c0 = block_cols(b)[0]
                    step = nc.vector.tensor_tensor_reduce(
                        out=prob[:, i % 2, h, c0:c0 + n], in0=ps[:, SCORE_BANK[group % 2], at:at + n],
                        in1=bias[:, i % 2, h, 256 - n:256], scale=1.0, scalar=-3.0e38, op0=ALU.add, op1=ALU.max,
                        accum_out=rmax[:, i % 2, h, b:b + 1])
                    at += n
                step.then_inc(s_read, 1)

            def neg_max(j, i, h):
                if h == 0 and i == 0:
                    dve.wait_ge(sink_set, j + 1)
                dve.wait_ge(s_read, 16 * j + 4 * i + 2 * h + 2)
                nc.vector.tensor_scalar(negm[:, i % 2, h, :], rmax[:, i % 2, h, :], sink_j[:, 2 * i + h:2 * i + h + 1],
                                        -1.0, ALU.max, ALU.mult).then_inc(negm_made, 1)

            def normalise(a, i, h):
                hd = 2 * a + h + 1
                dve.wait_ge(exp_made, hd)
                nc.vector.tensor_tensor(den[:, i % 2, h, :], rsum[:, i % 2, h, :], esink[:, i % 2, h, :],
                                        ALU.add).then_inc(den_made, 1)
                dve.wait_ge(den_made, hd)
                nc.vector.reciprocal(rden[:, i % 2, h, :], den[:, i % 2, h, :]).then_inc(rden_made, 1)
                dve.wait_ge(rden_made, hd)
                for b in range(TT):
                    c0 = block_cols(b)[0]
                    n = 128 if b == 0 else 256
                    step = nc.vector.tensor_scalar(prob[:, i % 2, h, c0:c0 + n], prob[:, i % 2, h, c0:c0 + n],
                                                   rden[:, i % 2, h, b:b + 1], None, ALU.mult)
                step.then_inc(p_made, 1)

            def pt_evac(b, y):
                n = 384 if y % 2 else 512
                dve.wait_ge(pt_hi_made, 4 * b + y + 1)
                nc.vector.tensor_tensor(pt_lo[:, y % 2, 0:n], ps[:, PT_BANK, 0:n], pt_hi[:, y % 2, 0:n].bitcast(F32),
                                        ALU.subtract).then_inc(pt_lo_made, 1)

            def o_evac(b, i):
                dve.wait_ge(o_hi_made, b + 1)
                nc.vector.tensor_tensor(ht_lo[:, i, :], ps[:, PV_BANK, :], ht_hi[:, i, :].bitcast(F32),
                                        ALU.subtract).then_inc(o_lo_made, 1)

            def add_parts(turn, n, third, off, banks, summed, added, norm):
                base = 16 * turn
                for t in range(TT):
                    if t < TT - 1:
                        dve.wait_ge(summed, 12 * turn + 3 * n + t + 1)
                    else:
                        dve.wait_ge(w_used, halves(third, off) + 2)
                    part = acc[:, t, n * 512:(n + 1) * 512]
                    nc.vector.tensor_tensor(part, part, ps[:, banks[t], :], ALU.add).then_inc(added, 1)
                    if norm:
                        dve.wait_ge(added, 4 + base + 4 * n + t + 1)
                        nc.vector.bn_stats(stats[:, t, 6 * n:6 * n + 6], part).then_inc(stat_made, 1)

            def attention(j, third, last):
                a = 4 * j
                split_lo(third, 2, 0)
                split_lo(third, 2, 1)
                for i in range(1, 4 if last else 5):
                    q_evac(a + i - 1, i - 1)
                    if i >= 3:
                        o_evac(a + i - 3, i - 3)
                    split_lo(third, i + 2, 0)
                    if i >= 2:
                        pt_evac(a + i - 2, 0)
                    scores(a + i - 1, i - 1, 0)
                    scores(a + i - 1, i - 1, 1)
                    neg_max(j, i - 1, 0)
                    if i >= 2:
                        pt_evac(a + i - 2, 1)
                    split_lo(third, i + 2, 1)
                    normalise(a + i - 1, i - 1, 0)
                    scores(a + i - 1, i - 1, 2)
                    if i >= 2:
                        pt_evac(a + i - 2, 2)
                    scores(a + i - 1, i - 1, 3)
                    neg_max(j, i - 1, 1)
                    normalise(a + i - 1, i - 1, 1)
                    if i >= 2:
                        pt_evac(a + i - 2, 3)
                if last:
                    q_evac(a + 3, 3)
                    o_evac(a + 1, 1)
                    split_lo(third, 6, 0)
                    pt_evac(a + 2, 0)
                    scores(a + 3, 3, 0)
                    scores(a + 3, 3, 1)
                    neg_max(j, 3, 0)
                    pt_evac(a + 2, 1)
                    normalise(a + 3, 3, 0)
                    scores(a + 3, 3, 2)
                    pt_evac(a + 2, 2)
                    scores(a + 3, 3, 3)
                    neg_max(j, 3, 1)
                    pt_evac(a + 2, 3)
                    o_evac(a + 2, 2)
                    normalise(a + 3, 3, 1)
                    split_lo(third, 6, 1)
                    for y in range(4):
                        pt_evac(a + 3, y)
                    o_evac(a + 3, 3)
                else:
                    kv_evac(j + 1)
                    o_evac(a + 2, 2)
                    pt_evac(a + 3, 0)
                    split_lo(third, 7, 0)
                    pt_evac(a + 3, 1)
                    pt_evac(a + 3, 2)
                    split_lo(third, 7, 1)
                    pt_evac(a + 3, 3)
                    o_evac(a + 3, 3)
                    v_evac(j + 1)
                dve.wait_ge(a_added, 16 * j + 4)
                first_row = 5 if last else 6
                banks = A_BANKS_LAST if last else A_BANKS
                add_parts(j, 0, third, first_row, banks[0], a_sum, a_added, last)
                for n in range(1, NN):
                    for h in range(2):
                        split_lo(third, first_row + n + 1, h)
                    add_parts(j, n, third, first_row + n, banks[n % 2], a_sum, a_added, last)

            def layer_norm(which, loaded):
                done = TT * which
                for t in range(TT):
                    dve.wait_ge(stat_made, 16 * which + 12 + t + 1)
                    nc.vector.bn_aggr(meanvar[:, t, :], stats[:, t, :]).then_inc(mean_made, 1)
                dve.wait_ge(loaded, 32)
                for t in range(TT):
                    dve.wait_ge(std_made, done + t + 1)
                    nc.vector.reciprocal(rstd[:, t:t + 1], std[:, t:t + 1]).then_inc(rstd_made, 1)
                    dve.wait_ge(mean_made, done + t + 1)
                    nc.vector.scalar_tensor_tensor(out=acc[:, t, :], in0=acc[:, t, :], scalar=meanvar[:, t, 0:1],
                                                   in1=lng[:, :], op0=ALU.subtract, op1=ALU.mult).then_inc(centered, 1)
                    dve.wait_ge(rstd_made, done + t + 1)
                    dve.wait_ge(centered, done + t + 1)
                    nc.vector.scalar_tensor_tensor(out=acc[:, t, :], in0=acc[:, t, :], scalar=rstd[:, t:t + 1],
                                                   in1=lnb[:, :], op0=ALU.mult, op1=ALU.add).then_inc(ln_made, 1)

            def ffn_group(g, third, last):
                for c in range(GC):
                    for u in (2 * c + 1, 2 * c + 2):
                        for h in range(2):
                            split_lo(third, u, h)
                    dve.wait_ge(w_used, halves(third, 2 * c + 1) + 2)
                    dve.wait_ge(sg_made, 4 * g + c + 1)
                    nc.vector.tensor_tensor(hm[:, :], sg[:, :], ps[:, 2 * c + 1, :], ALU.mult).then_inc(hm_made, 1)
                    dve.wait_ge(h_hi_made, 4 * g + c + 1)
                    nc.vector.tensor_tensor(ht_lo[:, c, :], hm[:, :], ht_hi[:, c, :].bitcast(F32),
                                            ALU.subtract).then_inc(h_lo_made, 1)
                dve.wait_ge(b_added, 16 * g + 4)
                for n in range(NN):
                    if not (last and n == NN - 1):
                        for h in range(2):
                            split_lo(third, 2 * GC + n + 1, h)
                    add_parts(g, n, third, 2 * GC + n, B_BANKS[n % 2], b_sum, b_added, last)

            xt_evac(0)
            for off in range(2):
                for h in range(2):
                    split_lo(0, off, h)
            kv_evac(0)
            v_evac(0)
            with dve.Fori(0, KVH - 1) as j:
                attention(j, 3 * j, False)
            attention(KVH - 1, 3 * (KVH - 1), True)
            layer_norm(0, ln1_in)
            xt_evac(1)
            with dve.Fori(0, NG - 1) as g:
                ffn_group(g, 4 * g + 12, False)
            ffn_group(NG - 1, 4 * (NG - 1) + 12, True)
            layer_norm(1, ln2_in)

        @block.tensor
        def _(pe):
            def transpose_rows(phase):
                for e in range(16):
                    t, q = divmod(e, 4)
                    if q == 0:
                        if phase == 0:
                            pe.wait_ge(x_in[t], 16)
                        else:
                            pe.wait_ge(ln_made, t + 1)
                    if e >= 8:
                        pe.wait_ge(xt_lo_made, 16 * phase + e - 7)
                    for k in range(4):
                        kk = 4 * q + k
                        step = nc.tensor.transpose(ps[:, e % 8, k * P:(k + 1) * P],
                                                   acc[:, t, kk * P:(kk + 1) * P], ident[:, :])
                    step.then_inc(xt_tr, 1)

            def column_step(third, off, k, bank):
                h, kk = divmod(k, 8)
                s = half_slot(off, h)
                if kk == 0:
                    pe.wait_ge(lo_made, halves(third, off) + h + 1)
                hi = w_hi[:, s, kk * P:(kk + 1) * P]
                lo = w_lo[:, s, kk * P:(kk + 1) * P]
                nc.tensor.matmul(ps[:, bank, :], hi, xt_lo[:, k, :], start=(k == 0), stop=False)
                nc.tensor.matmul(ps[:, bank, :], hi, xt_hi[:, k, :], start=False, stop=False)
                step = nc.tensor.matmul(ps[:, bank, :], lo, xt_hi[:, k, :], start=False, stop=(k == KD - 1))
                if kk == 7:
                    step.then_inc(w_used, 1)

            def row_step(third, off, kk, t, bank, summed):
                h, half_k = divmod(kk, 2)
                s = half_slot(off, h)
                if half_k == 0 and t == 0:
                    pe.wait_ge(lo_made, halves(third, off) + h + 1)
                hi = w_hi[:, s, half_k * 512:(half_k + 1) * 512]
                lo = w_lo[:, s, half_k * 512:(half_k + 1) * 512]
                tok = slice(t * P, (t + 1) * P)
                nc.tensor.matmul(ps[:, bank, :], ht_hi[:, kk, tok], lo, start=(kk == 0), stop=False)
                nc.tensor.matmul(ps[:, bank, :], ht_hi[:, kk, tok], hi, start=False, stop=False)
                step = nc.tensor.matmul(ps[:, bank, :], ht_lo[:, kk, tok], hi, start=False, stop=(kk == 3))
                if half_k == 1 and t == TT - 1:
                    step.then_inc(w_used, 1)
                elif kk == 3:
                    step.then_inc(summed, 1)

            def scores(a, i, j, group):
                h, half = divmod(group, 2)
                bank = SCORE_BANK[group % 2]
                if i == 0 and group == 0:
                    pe.wait_ge(k_lo_made, j + 1)
                    pe.wait_ge(a_added, 16 * j + 4)
                elif i > 0 or group >= 2:
                    pe.wait_ge(s_read, 4 * a + group - 1)
                if half == 0:
                    pe.wait_ge(q_lo_made, 2 * a + h + 1)
                at = 0
                for b in (2 * half, 2 * half + 1):
                    n = 128 if b == 0 else 256
                    keys = slice((b + 1) * P - n, (b + 1) * P)
                    q = q_st[:, h, b * P:(b + 1) * P]
                    nc.tensor.matmul(ps[:, bank, at:at + n], q, k_lo[:, keys], start=True, stop=False)
                    step = nc.tensor.matmul(ps[:, bank, at:at + n], q, k_hi[:, keys], start=False, stop=True)
                    at += n
                step.then_inc(s_done, 1)

            def transpose_p(b, i, y):
                h, half = divmod(y, 2)
                if half == 0:
                    pe.wait_ge(p_made, 2 * b + h + 1)
                if i > 0 or y > 0:
                    pe.wait_ge(pt_lo_made, 4 * b + y)
                at = 0
                for c in (2 * half, 2 * half + 1):
                    own = block_cols(c)[1]
                    step = nc.tensor.transpose(ps[:, PT_BANK, at:at + P], prob[:, i % 2, h, own:own + P], ident[:, :])
                    at += P
                    if c < TT - 1:
                        prev = block_cols(c + 1)[0]
                        step = nc.tensor.transpose(ps[:, PT_BANK, at:at + P], prob[:, i % 2, h, prev:prev + P],
                                                   ident[:, :])
                        at += P
                step.then_inc(pt_tr, 1)

            def p_times_v(b, i, j, y):
                h, half = divmod(y, 2)
                if y == 0:
                    if i == 0:
                        pe.wait_ge(v_lo_made, j + 1)
                    else:
                        pe.wait_ge(o_lo_made, b)
                pe.wait_ge(pt_lo_made, 4 * b + y + 1)
                cols = slice(64, 192) if h == 0 else slice(0, 128)
                at = 0
                for c in (2 * half, 2 * half + 1):
                    n = 256 if c < TT - 1 else 128
                    o = ps[:, PV_BANK, c * P:c * P + n]
                    vh, vl = v_hi[:, c, cols], v_lo[:, c, cols]
                    ph, pl = pt_hi[:, y % 2, at:at + n], pt_lo[:, y % 2, at:at + n]
                    nc.tensor.matmul(o, vl, ph, start=(y == 0 and c == 0), stop=False, skip_group_check=True)
                    nc.tensor.matmul(o, vh, pl, start=False, stop=False, skip_group_check=True)
                    step = nc.tensor.matmul(o, vh, ph, start=False, stop=(y == 3 and c == TT - 1), skip_group_check=True)
                    at += n
                step.then_inc(pv_done, 1)

            def transpose_v(m, groups):
                pe.wait_ge(kv_hi_made, m + 1)
                if groups is not None:
                    pe.wait_ge(pt_lo_made, groups)
                pe.sem_inc(waited_pe, 1)
                for c in range(TT):
                    step = nc.tensor.transpose(ps[:, PT_BANK, 64 * c:64 * c + 64], vt[:, c * P:(c + 1) * P],
                                               ident[0:64, 0:64])
                step.then_inc(v_tr, 1)

            def attention(j, third, last):
                a = 4 * j
                pe.wait_ge(a_added, 16 * j + 1)
                for k in range(KD):
                    column_step(third, 1, k, 0)
                for i in range(1, 4 if last else 5):
                    bank = i % 4
                    for k in range(KD):
                        column_step(third, 1 + i, k, bank)
                        if k == 3:
                            scores(a + i - 1, i - 1, j, 0)
                        if k == 4:
                            scores(a + i - 1, i - 1, j, 1)
                        if k == 8:
                            scores(a + i - 1, i - 1, j, 2)
                        if k == 9:
                            scores(a + i - 1, i - 1, j, 3)
                        if i >= 2:
                            if k == 1:
                                transpose_p(a + i - 2, i - 2, 0)
                            if k == 5:
                                p_times_v(a + i - 2, i - 2, j, 0)
                                transpose_p(a + i - 2, i - 2, 1)
                            if k == 9:
                                p_times_v(a + i - 2, i - 2, j, 1)
                                transpose_p(a + i - 2, i - 2, 2)
                            if k == 12:
                                p_times_v(a + i - 2, i - 2, j, 2)
                                transpose_p(a + i - 2, i - 2, 3)
                            if k == 15:
                                p_times_v(a + i - 2, i - 2, j, 3)
                if last:
                    row_units_last(j, third, a)
                else:
                    row_units(j, third, a)

            PART_0 = [(0, 0), (0, 1), (0, 2), (1, 0), (1, 1), (1, 2), (0, 3), (1, 3)]
            PART_0 += [(kk, t) for kk in (2, 3) for t in range(TT)]

            def row_units(j, third, a):
                for s, (kk, t) in enumerate(PART_0):
                    if (kk, t) == (0, 0):
                        pe.wait_ge(o_lo_made, 4 * j + 2)
                    if (kk, t) == (2, 0):
                        pe.wait_ge(o_lo_made, 4 * j + 3)
                    if (kk, t) == (0, 3):
                        pe.wait_ge(k_lo_made, j + 2)
                    if (kk, t) == (3, 0):
                        pe.wait_ge(o_lo_made, 4 * j + 4)
                    row_step(third, 6, kk, t, A_BANKS[0][t], a_sum)
                    if s == 0:
                        transpose_p(a + 3, 3, 0)
                    if s in (3, 6, 9):
                        p_times_v(a + 3, 3, j, s // 3 - 1)
                        transpose_p(a + 3, 3, s // 3)
                    if s == 11:
                        p_times_v(a + 3, 3, j, 3)
                    if s == 12:
                        transpose_v(j + 1, 16 * j + 16)
                pe.wait_ge(v_lo_made, j + 2)
                other_row_units(j, third, 6, A_BANKS)

            def row_units_last(j, third, a):
                for s, (kk, t) in enumerate(PART_0):
                    if t == 0:
                        pe.wait_ge(o_lo_made, 4 * j + kk + 1)
                    if (kk, t) == (0, 3):
                        pe.wait_ge(q_lo_made, 8 * j + 8)
                    row_step(third, 5, kk, t, A_BANKS_LAST[0][t], a_sum)
                    if s == 1:
                        transpose_p(a + 2, 2, 0)
                    if s == 3:
                        scores(a + 3, 3, j, 0)
                    if s == 4:
                        scores(a + 3, 3, j, 1)
                    if s == 5:
                        p_times_v(a + 2, 2, j, 0)
                        transpose_p(a + 2, 2, 1)
                    if s == 6:
                        scores(a + 3, 3, j, 2)
                    if s == 7:
                        p_times_v(a + 2, 2, j, 1)
                        transpose_p(a + 2, 2, 2)
                        scores(a + 3, 3, j, 3)
                        p_times_v(a + 2, 2, j, 2)
                        transpose_p(a + 2, 2, 3)
                        p_times_v(a + 2, 2, j, 3)
                    if s == 11:
                        transpose_p(a + 3, 3, 0)
                        for y in range(3):
                            p_times_v(a + 3, 3, j, y)
                            transpose_p(a + 3, 3, y + 1)
                        p_times_v(a + 3, 3, j, 3)
                other_row_units(j, third, 5, A_BANKS_LAST)

            def other_row_units(j, third, first, banks):
                for n in range(1, NN):
                    for kk in range(4):
                        for t in range(TT):
                            if kk == 0 and n >= 2:
                                pe.wait_ge(a_added, 16 * j + 4 + 4 * (n - 2) + t + 1)
                            row_step(third, first + n, kk, t, banks[n % 2][t], a_sum)

            def ffn_group(g, third):
                for c in range(GC):
                    for up in range(2):
                        if up == 0 and c == 0:
                            pe.wait_ge(b_added, 16 * g + 1)
                        if up == 0 and c == 2:
                            pe.wait_ge(b_added, 16 * g + 4)
                        for k in range(KD):
                            column_step(third, 2 * c + up, k, 2 * c + up)
                for n in range(NN):
                    for kk in range(4):
                        if n == 0:
                            pe.wait_ge(h_lo_made, 4 * g + max(kk + 1, 2))
                        for t in range(TT):
                            if kk == 0 and n >= 2:
                                pe.wait_ge(b_added, 16 * g + 4 + 4 * (n - 2) + t + 1)
                            row_step(third, 2 * GC + n, kk, t, B_BANKS[n % 2][t], b_sum)

            pe.wait_ge(consts, 2)
            transpose_rows(0)
            pe.wait_ge(xt_lo_made, 16)
            for k in range(KD):
                column_step(0, 0, k, 0)
            transpose_v(0, None)
            pe.wait_ge(k_lo_made, 1)
            pe.wait_ge(v_lo_made, 1)
            with pe.Fori(0, KVH - 1) as j:
                attention(j, 3 * j, False)
            attention(KVH - 1, 3 * (KVH - 1), True)
            transpose_rows(1)
            pe.wait_ge(xt_lo_made, 32)
            with pe.Fori(0, NG) as g:
                ffn_group(g, 4 * g + 12)


_INS = ["x", "a_w_in", "a_sinks", "a_w_out", "ln_g", "ln_b", "ffn_w_gate_up", "ffn_w_down"]


def kernel(**inputs):
    import numpy as _np
    import concourse.bacc as _bacc
    from concourse import mybir as _mybir
    from concourse.bass_utils import run_bass_kernel_spmd as _run

    nc = _bacc.Bacc("TRN2", target_bir_lowering=False, num_devices=1)
    arrays, args = {}, []
    for name in _INS:
        a = _np.ascontiguousarray(inputs[name])
        arrays[f"in_{name}"] = a
        args.append(nc.dram_tensor(f"in_{name}", a.shape, _mybir.dt.from_np(a.dtype), kind="ExternalInput").ap())
    shape = inputs["x"].shape
    result = nc.dram_tensor("out_rows", shape, _mybir.dt.float32, kind="ExternalOutput").ap()
    trunk_layer(nc, *args, result)
    r = _run(nc, [arrays], core_ids=[0])
    return r.results[0]["out_rows"]
```

```python
from contextlib import ExitStack

import concourse.bass as bass
from concourse import mybir

F32 = mybir.dt.float32
F32R = mybir.dt.float32r
I32 = mybir.dt.int32
ALU = mybir.AluOpType
ACT = mybir.ActivationFunctionType

P = 128
LN_EPS = 1e-5
DEPTH = 1
ALPHA = (2 * DEPTH) ** 0.25
HEAD_DIM = 64
N_HEADS = 32
GQA = 8
WINDOW = 128
MASKED = 1.0e30


def trunk_layer(nc, x, w_in, sinks, w_out, ln_g, ln_b, w_gu, w_dn, out):
    S, D = x.shape[1], x.shape[2]
    Q_DIM = N_HEADS * HEAD_DIM
    KV_DIM = (w_in.shape[2] - Q_DIM) // 2
    FF = w_dn.shape[1]
    TT = S // P
    KD = D // P
    NN = D // 512
    KVH = N_HEADS // GQA
    TPJ = GQA // 2
    GC = 4
    NG = FF // P // GC
    HS = 1024
    A_UNITS = TPJ + 1 + NN
    B_UNITS = 2 * GC + NN
    assert S == 512 and D == 2048 and FF % (P * GC) == 0 and A_UNITS == 9 and B_UNITS == 12
    SCALE = HEAD_DIM ** -0.5
    SLOPE = [2.0 ** (-8.0 * (r + 1) / N_HEADS) for r in range(GQA)]
    SLOPE_STEP = 2.0 ** (-8.0 * GQA / N_HEADS)

    x_rows = x.rearrange("o (t p) d -> (o p) t d", p=P)
    out_rows = out.rearrange("o (t p) d -> (o p) t d", p=P)
    win_v = w_in.rearrange("o (k p) m -> (o p) k m", p=P)
    wout_v = w_out.rearrange("o (k p) m -> (o p) k m", p=P)
    wgu_v = w_gu.rearrange("o (k p) m -> (o p) k m", p=P)
    wdn_v = w_dn.rearrange("o (k p) m -> (o p) k m", p=P)

    with ExitStack() as ctx:
        def sb(name, shape, dt=F32):
            return ctx.enter_context(nc.sbuf_tensor(name, shape, dt))

        def sem(name):
            return ctx.enter_context(nc.semaphore(name))

        xt_hi = sb("xt_hi", [P, KD, S], F32R)
        xt_lo = sb("xt_lo", [P, KD, S], F32R)
        acc = sb("acc", [P, TT, D])
        raw = sb("raw", [P, 3, 2 * HS])
        w_hi = sb("w_hi", [P, 3, HS], F32R)
        w_lo = sb("w_lo", [P, 3, HS], F32R)
        ht_hi = sb("ht_hi", [P, 4, S], F32R)
        ht_lo = sb("ht_lo", [P, 4, S], F32R)
        ident = sb("ident", [P, P])
        eps = sb("eps", [P, 1])
        stats = sb("stats", [P, TT, NN * 6])
        meanvar = sb("meanvar", [P, TT, 2])
        std = sb("std", [P, TT])
        rstd = sb("rstd", [P, TT])

        with ExitStack() as a_ctx:
            def sa(name, shape, dt=F32):
                return a_ctx.enter_context(nc.sbuf_tensor(name, shape, dt))

            k_hi = sa("k_hi", [P, S], F32R)
            k_lo = sa("k_lo", [P, S], F32R)
            v_hi = sa("v_hi", [P, TT, 192], F32R)
            v_lo = sa("v_lo", [P, TT, 192], F32R)
            vt = sa("vt", [HEAD_DIM, S])
            q_st = sa("q_st", [P, 2, S], F32R)
            bias = sa("bias", [P, 2, 2, 256])
            prob = sa("prob", [P, 2, 2, 896])
            pt_hi = sa("pt_hi", [P, 2, 512], F32R)
            pt_lo = sa("pt_lo", [P, 2, 512], F32R)
            dist = sa("dist", [P, 256])
            dist_i = sa("dist_i", [P, 256], I32)
            sink_all = sa("sink_all", [P, N_HEADS])
            sink_j = sa("sink_j", [P, GQA])
            rmax = sa("rmax", [P, 2, 2, TT])
            negm = sa("negm", [P, 2, 2, TT])
            esink = sa("esink", [P, 2, 2, TT])
            rsum = sa("rsum", [P, 2, 2, TT])
            den = sa("den", [P, 2, 2, TT])
            rden = sa("rden", [P, 2, 2, TT])
        with ExitStack() as b_ctx:
            def sb2(name, shape, dt=F32):
                return b_ctx.enter_context(nc.sbuf_tensor(name, shape, dt))

            lng = sb2("lng", [P, D])
            lnb = sb2("lnb", [P, D])
            sg = sb2("sg", [P, S])
            hm = sb2("hm", [P, S])

        ps = ctx.enter_context(nc.psum_tensor("ps", [P, 8, 512], F32))
        SCORE_BANK = (4, 5)
        PT_BANK, PV_BANK = 6, 7
        KV_BANK = 3
        B_BANKS = ([0, 1, 2, 3], [4, 5, 6, 7])

        x_in = [sem(f"x_in{t}") for t in range(TT)]
        raw_in = [sem(f"raw_in{s}") for s in range(3)]
        rawv_in = sem("rawv_in")
        sinks_in = sem("sinks_in")
        ln1_in = sem("ln1_in")
        ln2_in = sem("ln2_in")
        out_sent = sem("out_sent")
        consts = sem("consts")
        hi_made = sem("hi_made")
        lo_made = sem("lo_made")
        w_used = sem("w_used")
        xt_tr = sem("xt_tr")
        xt_hi_made = sem("xt_hi_made")
        xt_lo_made = sem("xt_lo_made")
        q_hi_made = sem("q_hi_made")
        q_lo_made = sem("q_lo_made")
        kv_hi_made = sem("kv_hi_made")
        k_lo_made = sem("k_lo_made")
        v_tr = sem("v_tr")
        v_hi_made = sem("v_hi_made")
        v_lo_made = sem("v_lo_made")
        sink_set = sem("sink_set")
        bias_set = sem("bias_set")
        dist_set = sem("dist_set")
        s_done = sem("s_done")
        s_read = sem("s_read")
        negm_made = sem("negm_made")
        exp_made = sem("exp_made")
        den_made = sem("den_made")
        rden_made = sem("rden_made")
        p_made = sem("p_made")
        pt_tr = sem("pt_tr")
        pt_hi_made = sem("pt_hi_made")
        pt_lo_made = sem("pt_lo_made")
        pv_done = sem("pv_done")
        o_hi_made = sem("o_hi_made")
        o_lo_made = sem("o_lo_made")
        a_sum = sem("a_sum")
        a_added = sem("a_added")
        b_sum = sem("b_sum")
        b_added = sem("b_added")
        stat_made = sem("stat_made")
        mean_made = sem("mean_made")
        std_made = sem("std_made")
        rstd_made = sem("rstd_made")
        centered = sem("centered")
        ln_made = sem("ln_made")
        sg_made = sem("sg_made")
        hm_made = sem("hm_made")
        h_hi_made = sem("h_hi_made")
        h_lo_made = sem("h_lo_made")

        waited_dve = sem("waited_dve")
        waited_pool = sem("waited_pool")
        waited_pe = sem("waited_pe")

        block = ctx.enter_context(nc.Block())

        def halves(third, off):
            return 6 * third + 2 * off

        def half_slot(off, h):
            return (2 * off + h) % 3

        def q_bank(i, last):
            return i if i < 3 or last else 0

        FIRST_HALF = [(0, 0), (0, 1), (0, 2), (1, 0), (1, 1), (1, 2), (0, 3), (1, 3)]
        TILE_ORDER = [(kk, t) for t in range(TT) for kk in range(2)]

        def block_cols(b):
            return max(256 * b - 128, 0), 256 * b

        @block.sync
        def _(sp):
            def load(third, off, src, wait=True):
                if wait:
                    sp.wait_ge(lo_made, halves(third, off) - 4)
                n = src.shape[2]
                dst = raw[:, off % 3, :].rearrange("p (k n) -> p k n", n=n)
                sp.dma_start(dst, src).then_inc(raw_in[off % 3], 16)

            def load_q(third, off, j, i):
                load(third, off, win_v[:, :, bass.ds(512 * j + P * i, P)], wait=not first_units(third, off))

            def first_units(third, off):
                return isinstance(third, int) and 3 * third + off < 3

            def load_kv(third, off, j):
                if not first_units(third, off):
                    sp.wait_ge(lo_made, halves(third, off) - 4)
                dst = raw[:, off % 3, :].rearrange("p (k n) -> p k n", n=P)
                sp.dma_start(dst[:, :, 0:64], win_v[:, :, bass.ds(Q_DIM + 64 * j, 64)]).then_inc(raw_in[off % 3], 16)
                sp.dma_start(dst[:, :, 64:128], win_v[:, :, bass.ds(Q_DIM + KV_DIM + 64 * j, 64)])\
                  .then_inc(rawv_in, 16)

            def load_wout(third, off, j, r):
                pair, part = divmod(r, 2)
                load(third, off, wout_v[:, bass.ds(4 * j + 2 * pair, 2), part * 1024:(part + 1) * 1024])

            for t in range(2):
                sp.dma_start(acc[:, t, :], x_rows[:, t, :]).then_inc(x_in[t], 16)
            load_kv(0, 0, 0)
            for t in range(2, TT):
                sp.dma_start(acc[:, t, :], x_rows[:, t, :]).then_inc(x_in[t], 16)
            load_q(0, 1, 0, 0)
            load_q(0, 2, 0, 1)
            with sp.Fori(0, KVH - 1) as j:
                third = 3 * j
                load_q(third, 3, j, 2)
                load_q(third, 4, j, 3)
                load_kv(third, 5, j + 1)
                for n in range(NN):
                    load_wout(third, 6 + n, j, n)
                load_q(third, 10, j, 4)
                load_q(third, 11, j, 5)
            j, third = KVH - 1, 3 * (KVH - 1)
            load_q(third, 3, j, 2)
            load_q(third, 4, j, 3)
            for n in range(NN):
                load_wout(third, 5 + n, j, n)
            sp.wait_ge(o_lo_made, TPJ * KVH)
            sp.dma_start(lng[:, :], ln_g[0, 0, :].partition_broadcast(P)).then_inc(ln1_in, 16)
            sp.dma_start(lnb[:, :], ln_b[0, 0, :].partition_broadcast(P)).then_inc(ln1_in, 16)
            with sp.Fori(0, NG) as g:
                third = 4 * g + 12
                for c in range(GC):
                    load(third, 2 * c, wgu_v[:, :, bass.ds(512 * g + P * c, P)])
                    load(third, 2 * c + 1, wgu_v[:, :, bass.ds(FF + 512 * g + P * c, P)])
                for n in range(NN):
                    load(third, 2 * GC + n, wdn_v[:, bass.ds(4 * g, 4), n * 512:(n + 1) * 512])
            sp.wait_ge(ln_made, TT)
            sp.dma_start(lng[:, :], ln_g[0, 1, :].partition_broadcast(P)).then_inc(ln2_in, 16)
            sp.dma_start(lnb[:, :], ln_b[0, 1, :].partition_broadcast(P)).then_inc(ln2_in, 16)
            for t in range(TT):
                sp.wait_ge(ln_made, TT + t + 1)
                sp.dma_start(out_rows[:, t, :], acc[:, t, :]).then_inc(out_sent, 16)
            sp.wait_ge(out_sent, 16 * TT)

        @block.gpsimd
        def _(pool):
            nc.gpsimd.memset(ident[:, :], 0.0).then_inc(consts, 1)
            pool.wait_ge(consts, 1)
            nc.gpsimd.affine_select(out=ident[:, :], in_=ident[:, :], compare_op=ALU.not_equal, fill=1.0,
                                    base=0, pattern=[[-1, P]], channel_multiplier=1).then_inc(consts, 1)
            nc.gpsimd.memset(eps[:, :], LN_EPS).then_inc(consts, 1)
            nc.gpsimd.memset(v_hi[:, :, :].bitcast(F32), 0.0).then_inc(consts, 1)
            nc.gpsimd.memset(v_lo[:, :, :].bitcast(F32), 0.0).then_inc(consts, 1)
            nc.gpsimd.iota(dist_i[:, :], pattern=[[-1, 256]], base=P, channel_multiplier=1).then_inc(consts, 1)
            pool.wait_ge(consts, 6)
            nc.gpsimd.tensor_copy(dist[:, :], dist_i[:, :]).then_inc(consts, 1)
            pool.wait_ge(consts, 7)
            nc.gpsimd.affine_select(out=dist[:, :], in_=dist[:, :], compare_op=ALU.is_ge, fill=MASKED,
                                    base=P, pattern=[[-1, 256]], channel_multiplier=1).then_inc(consts, 1)
            pool.wait_ge(consts, 8)
            nc.gpsimd.affine_select(out=dist[:, :], in_=dist[:, :], compare_op=ALU.is_ge, fill=MASKED,
                                    base=WINDOW - 1 - P, pattern=[[1, 256]], channel_multiplier=-1).then_inc(consts, 1)
            pool.wait_ge(consts, 9)
            pool.wait_ge(sinks_in, 16)

            def split_lo(third, off, h, wout=False):
                pool.wait_ge(hi_made, halves(third, off) + h + 1)
                whole = raw[:, off % 3, :]
                hi, lo = w_hi[:, half_slot(off, h), :].bitcast(F32), w_lo[:, half_slot(off, h), :]
                if wout:
                    nc.gpsimd.tensor_tensor(lo.rearrange("p (k n) -> p k n", n=512),
                                            whole.rearrange("p (k c n) -> p k c n", k=2, n=512)[:, :, h, :],
                                            hi.rearrange("p (k n) -> p k n", n=512), ALU.subtract).then_inc(lo_made, 1)
                else:
                    nc.gpsimd.tensor_tensor(lo, whole[:, h * HS:(h + 1) * HS], hi, ALU.subtract).then_inc(lo_made, 1)

            def biases(j, i):
                if i == 0:
                    pool.wait_ge(a_added, 32 * j + 1)
                    pool.sem_inc(waited_pool, 1)
                    nc.gpsimd.tensor_copy(sink_j[:, :], sink_all[:, bass.ds(GQA * j, GQA)]).then_inc(sink_set, 1)
                if i >= 2:
                    pool.wait_ge(s_read, 16 * j + 4 * (i - 1))
                    pool.sem_inc(waited_pool, 1)
                for h in range(2):
                    step = nc.gpsimd.tensor_scalar(bias[:, i % 2, h, :], dist[:, :], -SLOPE[2 * i + h], None, ALU.mult)
                step.then_inc(bias_set, 1)

            def attention(j, third, last):
                for i in range(TPJ):
                    split_lo(third, i + 2, 0, wout=(i == 3 and last))
                    biases(j, i)
                    split_lo(third, i + 2, 1, wout=(i == 3 and last))
                if not last:
                    pool.wait_ge(bias_set, TPJ * j + TPJ)
                    pool.sem_inc(waited_pool, 1)
                    nc.gpsimd.tensor_scalar(dist[:, :], dist[:, :], SLOPE_STEP, None, ALU.mult).then_inc(dist_set, 1)
                    pool.wait_ge(dist_set, j + 1)
                    for h in range(2):
                        split_lo(third, 6, h, wout=True)
                for r in range(4):
                    for h in range(2):
                        split_lo(third, (6 if last else 7) + r, h, wout=(r < 3))

            split_lo(0, 0, 0)
            split_lo(0, 0, 1)
            split_lo(0, 1, 0)
            split_lo(0, 1, 1)
            with pool.Fori(0, KVH - 1) as j:
                attention(j, 3 * j, False)
            attention(KVH - 1, 3 * (KVH - 1), True)

        @block.scalar
        def _(act):
            def split_hi(third, off, h, first=False, kv=None, wout=False):
                if h == 0:
                    act.wait_ge(raw_in[off % 3], 16 * (third + off // 3 + 1))
                    if kv is not None:
                        act.wait_ge(rawv_in, 16 * (kv + 1))
                if not first:
                    act.wait_ge(w_used, halves(third, off) + h - 2)
                if wout:
                    nc.scalar.activation(w_hi[:, half_slot(off, h), :].rearrange("p (k n) -> p k n", n=512),
                                         raw[:, off % 3, :].rearrange("p (k c n) -> p k c n", k=2, n=512)[:, :, h, :],
                                         ACT.Copy).then_inc(hi_made, 1)
                else:
                    nc.scalar.activation(w_hi[:, half_slot(off, h), :], raw[:, off % 3, h * HS:(h + 1) * HS],
                                         ACT.Copy).then_inc(hi_made, 1)

            def xt_evac(phase):
                for e in range(16):
                    t, q = divmod(e, 4)
                    act.wait_ge(xt_tr, 16 * phase + e + 1)
                    nc.scalar.activation(xt_hi[:, 4 * q:4 * q + 4, t * P:(t + 1) * P],
                                         ps[:, e % 8, :].rearrange("p (k n) -> p k n", n=P),
                                         ACT.Copy).then_inc(xt_hi_made, 1)

            def kv_evac(third, off, m):
                act.wait_ge(w_used, halves(third, off) + 2)
                nc.scalar.activation(k_hi[0:64, :], ps[0:64, KV_BANK, :], ACT.Copy)
                nc.scalar.activation(k_hi[64:128, :], ps[0:64, KV_BANK, :], ACT.Copy)
                nc.scalar.activation(vt[:, :], ps[64:128, KV_BANK, :], ACT.Copy).then_inc(kv_hi_made, 1)

            def v_evac(m):
                act.wait_ge(v_tr, m + 1)
                nc.scalar.activation(v_hi[:, :, 64:128], ps[:, PT_BANK, 0:256].rearrange("p (c d) -> p c d", d=64),
                                     ACT.Copy).then_inc(v_hi_made, 1)

            def q_evac(third, off, bank):
                act.wait_ge(w_used, halves(third, off) + 2)
                nc.scalar.activation(q_st[0:64, 0, :], ps[0:64, bank, :], ACT.Copy, scale=SCALE).then_inc(q_hi_made, 1)
                nc.scalar.activation(q_st[64:128, 1, :], ps[64:128, bank, :], ACT.Copy, scale=SCALE)\
                  .then_inc(q_hi_made, 1)

            def exps(a, i, h):
                act.wait_ge(negm_made, 2 * a + h + 1)
                nc.scalar.activation(esink[:, i % 2, h, :], negm[:, i % 2, h, :], ACT.Exp,
                                     bias=sink_j[:, 2 * i + h:2 * i + h + 1])
                for b in range(TT):
                    c0, own = block_cols(b)
                    c1 = own + 128
                    step = nc.scalar.activation(prob[:, i % 2, h, c0:c1], prob[:, i % 2, h, c0:c1], ACT.Exp,
                                                bias=negm[:, i % 2, h, b:b + 1],
                                                accum_out=rsum[:, i % 2, h, b:b + 1])
                step.then_inc(exp_made, 1)

            def pt_evac(b, y):
                n = 384 if y % 2 else 512
                if y >= 2:
                    act.wait_ge(pv_done, 4 * b + y - 1)
                act.wait_ge(pt_tr, 4 * b + y + 1)
                nc.scalar.activation(pt_hi[:, y % 2, 0:n], ps[:, PT_BANK, 0:n], ACT.Copy).then_inc(pt_hi_made, 1)

            def o_evac(b, i):
                act.wait_ge(pv_done, 4 * b + 4)
                nc.scalar.activation(ht_hi[:, i, :], ps[:, PV_BANK, :], ACT.Copy).then_inc(o_hi_made, 1)

            def attention(j, third, last):
                a = 4 * j
                split_hi(third, 2, 0)
                split_hi(third, 2, 1)
                for i in range(1, 6):
                    nxt = i + 2
                    kv = j + 1 if (nxt == 5 and not last) else None
                    wout = nxt >= (5 if last else 6)
                    if i <= 4:
                        q_evac(third, i, q_bank(i - 1, last))
                    elif not last:
                        kv_evac(third, 5, j + 1)
                    if i >= 2:
                        pt_evac(a + i - 2, 0)
                    if i >= 3:
                        o_evac(a + i - 3, i - 3)
                    split_hi(third, nxt, 0, kv=kv, wout=wout)
                    if i >= 2:
                        pt_evac(a + i - 2, 1)
                    if i <= 4:
                        exps(a + i - 1, i - 1, 0)
                    if i >= 2:
                        pt_evac(a + i - 2, 2)
                    if i <= 4:
                        exps(a + i - 1, i - 1, 1)
                    if i >= 2:
                        pt_evac(a + i - 2, 3)
                    split_hi(third, nxt, 1, wout=wout)
                o_evac(a + 3, 3)
                if not last:
                    v_evac(j + 1)
                for r in range(2 if last else 1, 4):
                    for h in range(2):
                        split_hi(third, (6 if last else 7) + r, h, wout=(r < 3))

            def layer_norm_std(which):
                for t in range(TT):
                    act.wait_ge(mean_made, TT * which + t + 1)
                    nc.scalar.activation(std[:, t:t + 1], meanvar[:, t, 1:2], ACT.Sqrt,
                                         bias=eps[:, :]).then_inc(std_made, 1)

            def ffn_group(g, third, last):
                for c in range(GC):
                    for h in range(2):
                        split_hi(third, 2 * c + 1, h)
                    act.wait_ge(w_used, halves(third, 2 * c) + 2)
                    nc.scalar.activation(sg[:, :], ps[:, 2 * c, :], ACT.Silu).then_inc(sg_made, 1)
                    for h in range(2):
                        split_hi(third, 2 * c + 2, h)
                    act.wait_ge(hm_made, 4 * g + c + 1)
                    nc.scalar.activation(ht_hi[:, c, :], hm[:, :], ACT.Copy).then_inc(h_hi_made, 1)
                for n in range(NN - 1 if last else NN):
                    for h in range(2):
                        split_hi(third, 2 * GC + n + 1, h)

            act.dma_start(sink_all[:, :], sinks[0, :].partition_broadcast(P)).then_inc(sinks_in, 16)
            xt_evac(0)
            split_hi(0, 0, 0, first=True, kv=0)
            split_hi(0, 0, 1, first=True)
            split_hi(0, 1, 0, first=True)
            split_hi(0, 1, 1)
            kv_evac(0, 0, 0)
            act.wait_ge(consts, 5)
            v_evac(0)
            with act.Fori(0, KVH - 1) as j:
                attention(j, 3 * j, False)
            attention(KVH - 1, 3 * (KVH - 1), True)
            layer_norm_std(0)
            xt_evac(1)
            with act.Fori(0, NG - 1) as g:
                ffn_group(g, 4 * g + 12, False)
            ffn_group(NG - 1, 4 * (NG - 1) + 12, True)
            layer_norm_std(1)

        @block.vector
        def _(dve):
            def split_lo(third, off, h):
                dve.wait_ge(hi_made, halves(third, off) + h + 1)
                nc.vector.tensor_tensor(w_lo[:, half_slot(off, h), :], raw[:, off % 3, h * HS:(h + 1) * HS],
                                        w_hi[:, half_slot(off, h), :].bitcast(F32), ALU.subtract).then_inc(lo_made, 1)

            def xt_evac(phase):
                for e in range(16):
                    t, q = divmod(e, 4)
                    dve.wait_ge(xt_hi_made, 16 * phase + e + 1)
                    nc.vector.tensor_tensor(xt_lo[:, 4 * q:4 * q + 4, t * P:(t + 1) * P],
                                            ps[:, e % 8, :].rearrange("p (k n) -> p k n", n=P),
                                            xt_hi[:, 4 * q:4 * q + 4, t * P:(t + 1) * P].bitcast(F32),
                                            ALU.subtract).then_inc(xt_lo_made, 1)

            def kv_evac(m):
                dve.wait_ge(kv_hi_made, m + 1)
                nc.vector.tensor_tensor(k_lo[0:64, :], ps[0:64, KV_BANK, :], k_hi[0:64, :].bitcast(F32), ALU.subtract)
                nc.vector.tensor_tensor(k_lo[64:128, :], ps[0:64, KV_BANK, :], k_hi[0:64, :].bitcast(F32),
                                        ALU.subtract).then_inc(k_lo_made, 1)

            def v_evac(m):
                dve.wait_ge(v_hi_made, m + 1)
                nc.vector.tensor_tensor(v_lo[:, :, 64:128], ps[:, PT_BANK, 0:256].rearrange("p (c d) -> p c d", d=64),
                                        v_hi[:, :, 64:128].bitcast(F32), ALU.subtract).then_inc(v_lo_made, 1)

            def q_evac(a, bank):
                for h in range(2):
                    top = slice(64 * h, 64 * h + 64)
                    other = slice(64 - 64 * h, 128 - 64 * h)
                    dve.wait_ge(q_hi_made, 2 * a + h + 1)
                    nc.vector.scalar_tensor_tensor(out=q_st[other, h, :], in0=ps[top, bank, :], scalar=SCALE,
                                                   in1=q_st[top, h, :].bitcast(F32), op0=ALU.mult,
                                                   op1=ALU.subtract).then_inc(q_lo_made, 1)

            def scores(a, i, group):
                h, half = divmod(group, 2)
                if group == 0:
                    dve.wait_ge(bias_set, a + 1)
                dve.wait_ge(s_done, 4 * a + group + 1)
                dve.sem_inc(waited_dve, 1)
                at = 0
                for b in (2 * half, 2 * half + 1):
                    n = 128 if b == 0 else 256
                    c0 = block_cols(b)[0]
                    step = nc.vector.tensor_tensor_reduce(
                        out=prob[:, i % 2, h, c0:c0 + n], in0=ps[:, SCORE_BANK[group % 2], at:at + n],
                        in1=bias[:, i % 2, h, 256 - n:256], scale=1.0, scalar=-3.0e38, op0=ALU.add, op1=ALU.max,
                        accum_out=rmax[:, i % 2, h, b:b + 1])
                    at += n
                step.then_inc(s_read, 1)

            def neg_max(j, i, h):
                if h == 0 and i == 0:
                    dve.wait_ge(sink_set, j + 1)
                dve.wait_ge(s_read, 16 * j + 4 * i + 2 * h + 2)
                nc.vector.tensor_scalar(negm[:, i % 2, h, :], rmax[:, i % 2, h, :], sink_j[:, 2 * i + h:2 * i + h + 1],
                                        -1.0, ALU.max, ALU.mult).then_inc(negm_made, 1)

            def normalise(a, i, h):
                hd = 2 * a + h + 1
                dve.wait_ge(exp_made, hd)
                nc.vector.tensor_tensor(den[:, i % 2, h, :], rsum[:, i % 2, h, :], esink[:, i % 2, h, :],
                                        ALU.add).then_inc(den_made, 1)
                dve.wait_ge(den_made, hd)
                nc.vector.reciprocal(rden[:, i % 2, h, :], den[:, i % 2, h, :]).then_inc(rden_made, 1)
                dve.wait_ge(rden_made, hd)
                for b in range(TT):
                    c0 = block_cols(b)[0]
                    n = 128 if b == 0 else 256
                    step = nc.vector.tensor_scalar(prob[:, i % 2, h, c0:c0 + n], prob[:, i % 2, h, c0:c0 + n],
                                                   rden[:, i % 2, h, b:b + 1], None, ALU.mult)
                step.then_inc(p_made, 1)

            def pt_evac(b, y):
                n = 384 if y % 2 else 512
                dve.wait_ge(pt_hi_made, 4 * b + y + 1)
                nc.vector.tensor_tensor(pt_lo[:, y % 2, 0:n], ps[:, PT_BANK, 0:n], pt_hi[:, y % 2, 0:n].bitcast(F32),
                                        ALU.subtract).then_inc(pt_lo_made, 1)

            def o_evac(b, i):
                dve.wait_ge(o_hi_made, b + 1)
                nc.vector.tensor_tensor(ht_lo[:, i, :], ps[:, PV_BANK, :], ht_hi[:, i, :].bitcast(F32),
                                        ALU.subtract).then_inc(o_lo_made, 1)

            def add_wout(j, third, last, r, h, t):
                n = 2 * (r % 2) + h
                across = last and r == 3
                if t == TT - 1:
                    dve.wait_ge(w_used, halves(third, (5 if last else 6) + r) + h + 1)
                elif across:
                    dve.wait_ge(a_sum, 24 * j + 18 + 2 * t + h + 1)
                else:
                    dve.wait_ge(a_sum, 24 * j + 6 * r + 3 * h + t + 1)
                part = acc[:, t, n * 512:(n + 1) * 512]
                bank = 4 + t if across and h else t
                nc.vector.tensor_tensor(part, part, ps[:, bank, :], ALU.add).then_inc(a_added, 1)
                if last and r >= 2:
                    at = 2 * t + h if across else 4 * h + t
                    dve.wait_ge(a_added, 4 + 32 * j + 8 * r + at + 1)
                    nc.vector.bn_stats(stats[:, t, 6 * n:6 * n + 6], part).then_inc(stat_made, 1)

            def attention(j, third, last):
                a = 4 * j
                for i in range(1, 6):
                    tile, b = i - 1, i - 2
                    r = i - 4 if last else i - 5
                    if i <= 4:
                        q_evac(a + tile, q_bank(tile, last))
                    elif not last:
                        kv_evac(j + 1)
                    if i >= 2:
                        pt_evac(a + b, 0)
                    if i >= 3:
                        o_evac(a + i - 3, i - 3)
                    if r == 0:
                        dve.wait_ge(a_added, 32 * j + 4)
                    if i <= 4:
                        scores(a + tile, tile, 0)
                        scores(a + tile, tile, 1)
                        neg_max(j, tile, 0)
                    if i >= 2:
                        pt_evac(a + b, 1)
                    if r >= 0:
                        for t in range(3):
                            add_wout(j, third, last, r, 0, t)
                    if i <= 4:
                        scores(a + tile, tile, 2)
                        scores(a + tile, tile, 3)
                        neg_max(j, tile, 1)
                        normalise(a + tile, tile, 0)
                    if r >= 0:
                        add_wout(j, third, last, r, 0, 3)
                    if i >= 2:
                        pt_evac(a + b, 2)
                    if r >= 0:
                        add_wout(j, third, last, r, 1, 0)
                        add_wout(j, third, last, r, 1, 1)
                    if i >= 2:
                        pt_evac(a + b, 3)
                    if r >= 0:
                        add_wout(j, third, last, r, 1, 2)
                    if i <= 4:
                        normalise(a + tile, tile, 1)
                    if r >= 0:
                        add_wout(j, third, last, r, 1, 3)
                o_evac(a + 3, 3)
                if not last:
                    v_evac(j + 1)
                for r in range(2 if last else 1, 4):
                    if last and r == 3:
                        for t in range(TT):
                            for h in range(2):
                                add_wout(j, third, last, r, h, t)
                    else:
                        for h in range(2):
                            for t in range(TT):
                                add_wout(j, third, last, r, h, t)

            def add_wdown(g, n, third, off, last):
                for t in range(TT):
                    if t < TT - 1:
                        dve.wait_ge(b_sum, 12 * g + 3 * n + t + 1)
                    else:
                        dve.wait_ge(w_used, halves(third, off) + 2)
                    part = acc[:, t, n * 512:(n + 1) * 512]
                    nc.vector.tensor_tensor(part, part, ps[:, B_BANKS[n % 2][t], :], ALU.add).then_inc(b_added, 1)
                    if last:
                        dve.wait_ge(b_added, 4 + 16 * g + 4 * n + t + 1)
                        nc.vector.bn_stats(stats[:, t, 6 * n:6 * n + 6], part).then_inc(stat_made, 1)

            def scale_residual(added):
                for t in range(TT):
                    nc.vector.tensor_scalar(acc[:, t, :], acc[:, t, :], ALPHA, None, ALU.mult).then_inc(added, 1)

            def layer_norm(which, loaded):
                done = TT * which
                for t in range(TT):
                    dve.wait_ge(stat_made, 8 + 2 * t + 2 if which == 0 else 16 + 12 + t + 1)
                    nc.vector.bn_aggr(meanvar[:, t, :], stats[:, t, :]).then_inc(mean_made, 1)
                dve.wait_ge(loaded, 32)
                for t in range(TT):
                    dve.wait_ge(std_made, done + t + 1)
                    nc.vector.reciprocal(rstd[:, t:t + 1], std[:, t:t + 1]).then_inc(rstd_made, 1)
                    dve.wait_ge(mean_made, done + t + 1)
                    nc.vector.scalar_tensor_tensor(out=acc[:, t, :], in0=acc[:, t, :], scalar=meanvar[:, t, 0:1],
                                                   in1=lng[:, :], op0=ALU.subtract, op1=ALU.mult).then_inc(centered, 1)
                    dve.wait_ge(rstd_made, done + t + 1)
                    dve.wait_ge(centered, done + t + 1)
                    nc.vector.scalar_tensor_tensor(out=acc[:, t, :], in0=acc[:, t, :], scalar=rstd[:, t:t + 1],
                                                   in1=lnb[:, :], op0=ALU.mult, op1=ALU.add).then_inc(ln_made, 1)

            def ffn_group(g, third, last):
                for c in range(GC):
                    for u in (2 * c + 1, 2 * c + 2):
                        for h in range(2):
                            split_lo(third, u, h)
                    dve.wait_ge(w_used, halves(third, 2 * c + 1) + 2)
                    dve.wait_ge(sg_made, 4 * g + c + 1)
                    nc.vector.tensor_tensor(hm[:, :], sg[:, :], ps[:, 2 * c + 1, :], ALU.mult).then_inc(hm_made, 1)
                    dve.wait_ge(h_hi_made, 4 * g + c + 1)
                    nc.vector.tensor_tensor(ht_lo[:, c, :], hm[:, :], ht_hi[:, c, :].bitcast(F32),
                                            ALU.subtract).then_inc(h_lo_made, 1)
                dve.wait_ge(b_added, 16 * g + 4)
                for n in range(NN):
                    if not (last and n == NN - 1):
                        for h in range(2):
                            split_lo(third, 2 * GC + n + 1, h)
                    add_wdown(g, n, third, 2 * GC + n, last)

            xt_evac(0)
            scale_residual(a_added)
            kv_evac(0)
            v_evac(0)
            with dve.Fori(0, KVH - 1) as j:
                attention(j, 3 * j, False)
            attention(KVH - 1, 3 * (KVH - 1), True)
            layer_norm(0, ln1_in)
            xt_evac(1)
            scale_residual(b_added)
            dve.wait_ge(lo_made, halves(12, 0) + 2)
            with dve.Fori(0, NG - 1) as g:
                ffn_group(g, 4 * g + 12, False)
            ffn_group(NG - 1, 4 * (NG - 1) + 12, True)
            layer_norm(1, ln2_in)

        @block.tensor
        def _(pe):
            def transpose_rows(phase):
                for e in range(16):
                    t, q = divmod(e, 4)
                    if q == 0:
                        if phase == 0:
                            pe.wait_ge(x_in[t], 16)
                        else:
                            pe.wait_ge(ln_made, t + 1)
                    if e >= 8:
                        pe.wait_ge(xt_lo_made, 16 * phase + e - 7)
                    for k in range(4):
                        kk = 4 * q + k
                        step = nc.tensor.transpose(ps[:, e % 8, k * P:(k + 1) * P],
                                                   acc[:, t, kk * P:(kk + 1) * P], ident[:, :])
                    step.then_inc(xt_tr, 1)

            def column_step(third, off, k, bank):
                h, kk = divmod(k, 8)
                s = half_slot(off, h)
                if kk == 0:
                    pe.wait_ge(lo_made, halves(third, off) + h + 1)
                hi = w_hi[:, s, kk * P:(kk + 1) * P]
                lo = w_lo[:, s, kk * P:(kk + 1) * P]
                nc.tensor.matmul(ps[:, bank, :], hi, xt_lo[:, k, :], start=(k == 0), stop=False)
                nc.tensor.matmul(ps[:, bank, :], hi, xt_hi[:, k, :], start=False, stop=False)
                step = nc.tensor.matmul(ps[:, bank, :], lo, xt_hi[:, k, :], start=False, stop=(k == KD - 1))
                if kk == 7:
                    step.then_inc(w_used, 1)

            def row_products(s, wk, kk, t, bank, first, last):
                hi = w_hi[:, s, wk * 512:(wk + 1) * 512]
                lo = w_lo[:, s, wk * 512:(wk + 1) * 512]
                tok = slice(t * P, (t + 1) * P)
                nc.tensor.matmul(ps[:, bank, :], ht_hi[:, kk, tok], lo, start=first, stop=False)
                nc.tensor.matmul(ps[:, bank, :], ht_hi[:, kk, tok], hi, start=False, stop=False)
                return nc.tensor.matmul(ps[:, bank, :], ht_lo[:, kk, tok], hi, start=False, stop=last)

            def wdown_step(g, third, n, kk, t):
                off = 2 * GC + n
                h, wk = divmod(kk, 2)
                if wk == 0 and t == 0:
                    pe.wait_ge(lo_made, halves(third, off) + h + 1)
                if kk == 0 and n >= 2:
                    pe.wait_ge(b_added, 16 * g + 4 + 4 * (n - 2) + t + 1)
                step = row_products(half_slot(off, h), wk, kk, t, B_BANKS[n % 2][t], kk == 0, kk == 3)
                if wk == 1 and t == TT - 1:
                    step.then_inc(w_used, 1)
                elif kk == 3:
                    step.then_inc(b_sum, 1)

            def wout_step(j, third, last, r, h, kk, t):
                off = (5 if last else 6) + r
                across = last and r == 3
                bank = 4 + t if across and h else t
                if kk == 0 and t == 0:
                    pe.wait_ge(lo_made, halves(third, off) + h + 1)
                if kk == 0 and across and h == 0:
                    pe.wait_ge(a_added, 32 * j + 8 * r + t + 1)
                elif kk == 0 and not across and (r, h) != (0, 0):
                    pe.wait_ge(a_added, 32 * j + 8 * r + 4 * h + t + 1)
                step = row_products(half_slot(off, h), kk, 2 * (r // 2) + kk, t, bank, kk == 0, kk == 1)
                if kk == 1 and t == TT - 1:
                    step.then_inc(w_used, 1)
                elif kk == 1:
                    step.then_inc(a_sum, 1)

            def scores(a, i, j, group):
                h, half = divmod(group, 2)
                bank = SCORE_BANK[group % 2]
                if i == 0 and group == 0:
                    pe.wait_ge(k_lo_made, j + 1)
                if i > 0 or group >= 2:
                    pe.wait_ge(s_read, 4 * a + group - 1)
                if half == 0:
                    pe.wait_ge(q_lo_made, 2 * a + h + 1)
                at = 0
                for b in (2 * half, 2 * half + 1):
                    n = 128 if b == 0 else 256
                    keys = slice((b + 1) * P - n, (b + 1) * P)
                    q = q_st[:, h, b * P:(b + 1) * P]
                    nc.tensor.matmul(ps[:, bank, at:at + n], q, k_lo[:, keys], start=True, stop=False)
                    step = nc.tensor.matmul(ps[:, bank, at:at + n], q, k_hi[:, keys], start=False, stop=True)
                    at += n
                step.then_inc(s_done, 1)

            def transpose_p(b, i, j, y):
                h, half = divmod(y, 2)
                if half == 0:
                    pe.wait_ge(p_made, 2 * b + h + 1)
                if i > 0 or y > 0:
                    pe.wait_ge(pt_lo_made, 4 * b + y)
                else:
                    pe.wait_ge(v_lo_made, j + 1)
                at = 0
                for c in (2 * half, 2 * half + 1):
                    own = block_cols(c)[1]
                    step = nc.tensor.transpose(ps[:, PT_BANK, at:at + P], prob[:, i % 2, h, own:own + P], ident[:, :])
                    at += P
                    if c < TT - 1:
                        prev = block_cols(c + 1)[0]
                        step = nc.tensor.transpose(ps[:, PT_BANK, at:at + P], prob[:, i % 2, h, prev:prev + P],
                                                   ident[:, :])
                        at += P
                step.then_inc(pt_tr, 1)

            def p_times_v(b, i, j, y):
                h, half = divmod(y, 2)
                if y == 0:
                    if i > 0:
                        pe.wait_ge(o_lo_made, b)
                pe.wait_ge(pt_lo_made, 4 * b + y + 1)
                cols = slice(64, 192) if h == 0 else slice(0, 128)
                at = 0
                for c in (2 * half, 2 * half + 1):
                    n = 256 if c < TT - 1 else 128
                    o = ps[:, PV_BANK, c * P:c * P + n]
                    vh, vl = v_hi[:, c, cols], v_lo[:, c, cols]
                    ph, pl = pt_hi[:, y % 2, at:at + n], pt_lo[:, y % 2, at:at + n]
                    nc.tensor.matmul(o, vl, ph, start=(y == 0 and c == 0), stop=False, skip_group_check=True)
                    nc.tensor.matmul(o, vh, pl, start=False, stop=False, skip_group_check=True)
                    step = nc.tensor.matmul(o, vh, ph, start=False, stop=(y == 3 and c == TT - 1), skip_group_check=True)
                    at += n
                step.then_inc(pv_done, 1)

            def transpose_v(m, groups):
                pe.wait_ge(kv_hi_made, m + 1)
                if groups is not None:
                    pe.wait_ge(pt_lo_made, groups)
                pe.sem_inc(waited_pe, 1)
                for c in range(TT):
                    step = nc.tensor.transpose(ps[:, PT_BANK, 64 * c:64 * c + 64], vt[:, c * P:(c + 1) * P],
                                               ident[0:64, 0:64])
                step.then_inc(v_tr, 1)

            def beside(k, i, j):
                tile, b = i - 1, i - 2
                if 0 <= tile < TPJ and k in (3, 4, 6, 7):
                    scores(4 * j + tile, tile, j, (3, 4, 6, 7).index(k))
                if b >= 0:
                    if k in (5, 9, 12, 15):
                        p_times_v(4 * j + b, b, j, (5, 9, 12, 15).index(k))
                    if k in (1, 5, 9, 12):
                        transpose_p(4 * j + b, b, j, (1, 5, 9, 12).index(k))

            def attention(j, third, last):
                pe.wait_ge(a_added, 32 * j + 1)
                for k in range(KD):
                    column_step(third, 1, k, q_bank(0, last))
                pe.wait_ge(a_added, 32 * j + 4)
                for i in range(1, 4 if last else 5):
                    for k in range(KD):
                        column_step(third, 1 + i, k, KV_BANK if i == 4 else q_bank(i, last))
                        beside(k, i, j)
                for r in range(4):
                    i = r + (4 if last else 5)
                    if r == 2:
                        pe.wait_ge(o_lo_made, 4 * j + 4)
                    if last and r == 3:
                        pe.wait_ge(lo_made, halves(third, 5 + r) + 2)
                        for t in range(TT):
                            for h in range(2):
                                for kk in range(2):
                                    wout_step(j, third, last, r, h, kk, t)
                        continue
                    for h in range(2):
                        for s, (kk, t) in enumerate(FIRST_HALF if (r, h) == (0, 0) else TILE_ORDER):
                            if (r, h) == (0, 0) and (kk, t) == (0, 0):
                                pe.wait_ge(o_lo_made, 4 * j + 1)
                            if (r, h) == (0, 0) and (kk, t) == (1, 0):
                                pe.wait_ge(o_lo_made, 4 * j + 2)
                            if (r, h) == (0, 0) and (kk, t) == (0, 3):
                                if last:
                                    pe.wait_ge(q_lo_made, 8 * j + 8)
                                else:
                                    pe.wait_ge(k_lo_made, j + 2)
                            wout_step(j, third, last, r, h, kk, t)
                            if i <= 5:
                                beside(8 * h + s, i, j)
                            if not last and r == 1 and 8 * h + s == 2:
                                transpose_v(j + 1, 16 * j + 16)

            def ffn_group(g, third):
                for c in range(GC):
                    for up in range(2):
                        if up == 0 and c == 0:
                            pe.wait_ge(b_added, 16 * g + 1)
                        if up == 0 and c == 2:
                            pe.wait_ge(b_added, 16 * g + 4)
                        for k in range(KD):
                            column_step(third, 2 * c + up, k, 2 * c + up)
                for n in range(NN):
                    for kk in range(4):
                        if n == 0:
                            pe.wait_ge(h_lo_made, 4 * g + max(kk + 1, 2))
                        for t in range(TT):
                            wdown_step(g, third, n, kk, t)

            pe.wait_ge(consts, 2)
            transpose_rows(0)
            pe.wait_ge(xt_lo_made, 16)
            for k in range(KD):
                column_step(0, 0, k, KV_BANK)
            transpose_v(0, None)
            pe.wait_ge(k_lo_made, 1)
            pe.wait_ge(v_lo_made, 1)
            with pe.Fori(0, KVH - 1) as j:
                attention(j, 3 * j, False)
            attention(KVH - 1, 3 * (KVH - 1), True)
            transpose_rows(1)
            pe.wait_ge(xt_lo_made, 32)
            with pe.Fori(0, NG) as g:
                ffn_group(g, 4 * g + 12)


_INS = ["x", "a_w_in", "a_sinks", "a_w_out", "ln_g", "ln_b", "ffn_w_gate_up", "ffn_w_down"]


def kernel(**inputs):
    import numpy as _np
    import concourse.bacc as _bacc
    from concourse import mybir as _mybir
    from concourse.bass_utils import run_bass_kernel_spmd as _run

    nc = _bacc.Bacc("TRN2", target_bir_lowering=False, num_devices=1)
    arrays, args = {}, []
    for name in _INS:
        a = _np.ascontiguousarray(inputs[name])
        arrays[f"in_{name}"] = a
        args.append(nc.dram_tensor(f"in_{name}", a.shape, _mybir.dt.from_np(a.dtype), kind="ExternalInput").ap())
    shape = inputs["x"].shape
    result = nc.dram_tensor("out_rows", shape, _mybir.dt.float32, kind="ExternalOutput").ap()
    trunk_layer(nc, *args, result)
    r = _run(nc, [arrays], core_ids=[0])
    return r.results[0]["out_rows"]
```

```python
from contextlib import ExitStack

import concourse.bass as bass
from concourse import mybir

F32 = mybir.dt.float32
F32R = mybir.dt.float32r
I32 = mybir.dt.int32
ALU = mybir.AluOpType
ACT = mybir.ActivationFunctionType

P = 128
LN_EPS = 1e-5
DEPTH = 1
ALPHA = (2 * DEPTH) ** 0.25
HEAD_DIM = 64
N_HEADS = 32
GQA = 8
WINDOW = 128
MASKED = 1.0e30


def trunk_layer(nc, x, w_in, sinks, w_out, ln_g, ln_b, w_gu, w_dn, out):
    S, D = x.shape[1], x.shape[2]
    Q_DIM = N_HEADS * HEAD_DIM
    KV_DIM = (w_in.shape[2] - Q_DIM) // 2
    FF = w_dn.shape[1]
    TT = S // P
    KD = D // P
    NN = D // 512
    KVH = N_HEADS // GQA
    TPJ = GQA // 2
    GC = 4
    NG = FF // P // GC
    HS = 1024
    A_UNITS = TPJ + 1 + NN
    B_UNITS = 2 * GC + NN
    assert S == 512 and D == 2048 and FF % (P * GC) == 0 and A_UNITS == 9 and B_UNITS == 12
    SCALE = HEAD_DIM ** -0.5
    SLOPE = [2.0 ** (-8.0 * (r + 1) / N_HEADS) for r in range(GQA)]
    SLOPE_STEP = 2.0 ** (-8.0 * GQA / N_HEADS)

    x_rows = x.rearrange("o (t p) d -> (o p) t d", p=P)
    out_rows = out.rearrange("o (t p) d -> (o p) t d", p=P)
    win_v = w_in.rearrange("o (k p) m -> (o p) k m", p=P)
    wout_v = w_out.rearrange("o (k p) m -> (o p) k m", p=P)
    wgu_v = w_gu.rearrange("o (k p) m -> (o p) k m", p=P)
    wdn_v = w_dn.rearrange("o (k p) m -> (o p) k m", p=P)

    with ExitStack() as ctx:
        def sb(name, shape, dt=F32):
            return ctx.enter_context(nc.sbuf_tensor(name, shape, dt))

        def sem(name):
            return ctx.enter_context(nc.semaphore(name))

        xt_hi = sb("xt_hi", [P, KD, S], F32R)
        xt_lo = sb("xt_lo", [P, KD, S], F32R)
        acc = sb("acc", [P, TT, D])
        raw = sb("raw", [P, 3, 2 * HS])
        w_hi = sb("w_hi", [P, 3, HS], F32R)
        w_lo = sb("w_lo", [P, 3, HS], F32R)
        ht_hi = sb("ht_hi", [P, 4, S], F32R)
        ht_lo = sb("ht_lo", [P, 4, S], F32R)
        ident = sb("ident", [P, P])
        eps = sb("eps", [P, 1])
        stats = sb("stats", [P, TT, NN * 6])
        meanvar = sb("meanvar", [P, TT, 2])
        std = sb("std", [P, TT])
        rstd = sb("rstd", [P, TT])
        shift = sb("shift", [P, TT])
        ln1_kp = sb("ln1_kp", [2 * KD, P])
        ln1_pk = sb("ln1_pk", [P, 2 * KD])

        with ExitStack() as a_ctx:
            def sa(name, shape, dt=F32):
                return a_ctx.enter_context(nc.sbuf_tensor(name, shape, dt))

            k_hi = sa("k_hi", [P, S], F32R)
            k_lo = sa("k_lo", [P, S], F32R)
            v_st = sa("v_st", [P, TT, 2 * HEAD_DIM], F32R)
            o_sum = sa("o_sum", [P, S])
            vt = sa("vt", [HEAD_DIM, S])
            q_st = sa("q_st", [P, 2, S], F32R)
            bias = sa("bias", [P, 2, 2, 256])
            prob = sa("prob", [P, 2, 2, 896])
            pt_hi = sa("pt_hi", [P, 2, 512], F32R)
            pt_lo = sa("pt_lo", [P, 2, 512], F32R)
            dist = sa("dist", [P, 256])
            dist_i = sa("dist_i", [P, 256], I32)
            sink_all = sa("sink_all", [P, N_HEADS])
            sink_j = sa("sink_j", [P, GQA])
            rmax = sa("rmax", [P, 2, 2, TT])
            negm = sa("negm", [P, 2, 2, TT])
            esink = sa("esink", [P, 2, 2, TT])
            rsum = sa("rsum", [P, 2, 2, TT])
            den = sa("den", [P, 2, 2, TT])
            rden = sa("rden", [P, 2, 2, TT])
        with ExitStack() as b_ctx:
            def sb2(name, shape, dt=F32):
                return b_ctx.enter_context(nc.sbuf_tensor(name, shape, dt))

            lng = sb2("lng", [P, D])
            lnb = sb2("lnb", [P, D])
            sg = sb2("sg", [P, S])
            hm = sb2("hm", [P, S])
            x1t = sb2("x1t", [P, 8, S])

        ps = ctx.enter_context(nc.psum_tensor("ps", [P, 8, 512], F32))
        SCORE_BANK = (4, 5)
        PT_BANK, PV_BANK = 6, 7
        KV_BANK = 3
        B_BANKS = ([0, 1, 2, 3], [4, 5, 6, 7])

        x_in = [sem(f"x_in{t}") for t in range(TT)]
        raw_in = [sem(f"raw_in{s}") for s in range(3)]
        kv0_in = sem("kv0_in")
        rawv_in = sem("rawv_in")
        sinks_in = sem("sinks_in")
        lnk_in = sem("lnk_in")
        lnk_tr = sem("lnk_tr")
        lnk_made = sem("lnk_made")
        ln1_in = sem("ln1_in")
        ln2_in = sem("ln2_in")
        out_sent = sem("out_sent")
        consts = sem("consts")
        hi_made = sem("hi_made")
        lo_made = sem("lo_made")
        w_used = sem("w_used")
        xt_tr = sem("xt_tr")
        xt_hi_made = sem("xt_hi_made")
        xt_lo_made = sem("xt_lo_made")
        q_hi_made = sem("q_hi_made")
        q_lo_made = sem("q_lo_made")
        vt_made = sem("vt_made")
        k_hi_made = sem("k_hi_made")
        k_lo_made = sem("k_lo_made")
        v_tr = sem("v_tr")
        v_hi_made = sem("v_hi_made")
        v_lo_made = sem("v_lo_made")
        sink_set = sem("sink_set")
        bias_set = sem("bias_set")
        dist_set = sem("dist_set")
        s_done = sem("s_done")
        s_read = sem("s_read")
        negm_made = sem("negm_made")
        exp_made = sem("exp_made")
        den_made = sem("den_made")
        rden_made = sem("rden_made")
        p_made = sem("p_made")
        pt_tr = sem("pt_tr")
        pt_hi_made = sem("pt_hi_made")
        pt_lo_made = sem("pt_lo_made")
        pv_done = sem("pv_done")
        o_part_made = sem("o_part_made")
        o_made = sem("o_made")
        o_hi_made = sem("o_hi_made")
        o_lo_made = sem("o_lo_made")
        a_sum = sem("a_sum")
        a_added = sem("a_added")
        b_sum = sem("b_sum")
        b_added = sem("b_added")
        stat_made = sem("stat_made")
        mean_made = sem("mean_made")
        std_made = sem("std_made")
        rstd_made = sem("rstd_made")
        shift_made = sem("shift_made")
        norm_act = sem("norm_act")
        norm_dve = sem("norm_dve")
        x1_tr = sem("x1_tr")
        x1_made = sem("x1_made")
        x1_hi_made = sem("x1_hi_made")
        x1_lo_dve = sem("x1_lo_dve")
        x1_lo_pool = sem("x1_lo_pool")
        gained = sem("gained")
        centered = sem("centered")
        ln_made = sem("ln_made")
        norm_cols = sem("norm_cols")
        ln_pool = sem("ln_pool")
        sg_made = sem("sg_made")
        hm_made = sem("hm_made")
        h_hi_made = sem("h_hi_made")
        h_lo_made = sem("h_lo_made")

        waited_dve = sem("waited_dve")
        waited_pool = sem("waited_pool")
        waited_pe = sem("waited_pe")

        block = ctx.enter_context(nc.Block())

        def halves(third, off):
            return 6 * third + 2 * off

        def half_slot(off, h):
            return (2 * off + h) % 3

        def q_bank(i, last):
            return i if i < 3 or last else 0

        DVE_COLS = 1152
        PIECES = [(0, 640), (640, DVE_COLS)]
        FILL = 20

        XT_BANKS = [0, 1, 2, 3, 4, 5, 6, 7, 0, 1, 2, 4, 5, 6, 7, 0]

        X1_GROUPS = KD // 2
        X1_BANKS = ([0, 1, 4, 5, 2, 6, 3, 7], [4, 5, 2, 6, 3, 7, 4, 5])
        PAIR = 2 * P

        def x1_group(buf, pair, q):
            return buf[:, 2 * q:2 * q + 2, pair * PAIR:(pair + 1) * PAIR]

        FIRST_HALF = [(0, 0), (0, 1), (0, 2), (1, 0), (1, 1), (1, 2), (0, 3), (1, 3)]
        TILE_ORDER = [(kk, t) for t in range(TT) for kk in range(2)]

        def block_cols(b):
            return max(256 * b - 128, 0), 256 * b

        @block.sync
        def _(sp):
            def load(third, off, src, wait=True):
                if wait:
                    sp.wait_ge(lo_made, halves(third, off) - 4)
                n = src.shape[2]
                dst = raw[:, off % 3, :].rearrange("p (k n) -> p k n", n=n)
                sp.dma_start(dst, src).then_inc(raw_in[off % 3], 16)

            def load_q(third, off, j, i):
                load(third, off, win_v[:, :, bass.ds(512 * j + P * i, P)], wait=not first_units(third, off))

            def first_units(third, off):
                return isinstance(third, int) and 3 * third + off < 3

            def load_kv(third, off, j):
                sp.wait_ge(lo_made, halves(third, off) - 4)
                dst = raw[:, off % 3, :].rearrange("p (k n) -> p k n", n=P)
                sp.dma_start(dst[:, :, 0:64], win_v[:, :, bass.ds(Q_DIM + 64 * j, 64)]).then_inc(raw_in[off % 3], 16)
                sp.dma_start(dst[:, :, 64:128], win_v[:, :, bass.ds(Q_DIM + KV_DIM + 64 * j, 64)])\
                  .then_inc(rawv_in, 16)

            def load_wout(third, off, j, r):
                pair, part = divmod(r, 2)
                load(third, off, wout_v[:, bass.ds(4 * j + 2 * pair, 2), part * 1024:(part + 1) * 1024])

            for t in range(TT):
                sp.dma_start(acc[:, t, :], x_rows[:, t, :]).then_inc(x_in[t], 16)
                if t < 2:
                    dst = raw[:, 0, t * HS:(t + 1) * HS].rearrange("p (k n) -> p k n", n=P)
                    src = win_v[:, t * KD // 2:(t + 1) * KD // 2, :]
                    sp.dma_start(dst[:, :, 0:64], src[:, :, Q_DIM:Q_DIM + 64]).then_inc(raw_in[0] if t else kv0_in, 16)
                    sp.dma_start(dst[:, :, 64:128], src[:, :, Q_DIM + KV_DIM:Q_DIM + KV_DIM + 64])\
                      .then_inc(rawv_in if t else kv0_in, 16)
            load_q(0, 1, 0, 0)
            load_q(0, 2, 0, 1)
            with sp.Fori(0, KVH - 1) as j:
                third = 3 * j
                load_q(third, 3, j, 2)
                load_q(third, 4, j, 3)
                load_kv(third, 5, j + 1)
                for n in range(NN):
                    load_wout(third, 6 + n, j, n)
                load_q(third, 10, j, 4)
                load_q(third, 11, j, 5)
            j, third = KVH - 1, 3 * (KVH - 1)
            load_q(third, 3, j, 2)
            load_q(third, 4, j, 3)
            for n in range(NN):
                load_wout(third, 5 + n, j, n)
            sp.wait_ge(o_lo_made, TPJ * KVH)
            sp.dma_start(lng[:, :], ln_g[0, 0, :].partition_broadcast(P)).then_inc(ln1_in, 16)
            sp.dma_start(lnb[:, :], ln_b[0, 0, :].partition_broadcast(P)).then_inc(ln1_in, 16)
            with sp.Fori(0, NG) as g:
                third = 4 * g + 12
                for c in range(GC):
                    load(third, 2 * c, wgu_v[:, :, bass.ds(512 * g + P * c, P)])
                    load(third, 2 * c + 1, wgu_v[:, :, bass.ds(FF + 512 * g + P * c, P)])
                for n in range(NN):
                    load(third, 2 * GC + n, wdn_v[:, bass.ds(4 * g, 4), n * 512:(n + 1) * 512])
            sp.wait_ge(b_added, TT)
            sp.dma_start(lng[:, :], ln_g[0, 1, :].partition_broadcast(P)).then_inc(ln2_in, 16)
            sp.dma_start(lnb[:, :], ln_b[0, 1, :].partition_broadcast(P)).then_inc(ln2_in, 16)
            for t in range(TT):
                for i, (lo, hi) in enumerate(PIECES if t == TT - 1 else [(0, DVE_COLS)]):
                    sp.wait_ge(ln_made, t + i + 1)
                    sp.dma_start(out_rows[:, t, lo:hi], acc[:, t, lo:hi]).then_inc(out_sent, 16)
                sp.wait_ge(ln_pool, t + 1)
                sp.dma_start(out_rows[:, t, DVE_COLS:D], acc[:, t, DVE_COLS:D]).then_inc(out_sent, 16)
            sp.wait_ge(out_sent, 16 * (2 * TT + 1))

        @block.gpsimd
        def _(pool):
            nc.gpsimd.memset(ident[:, :], 0.0).then_inc(consts, 1)
            pool.wait_ge(consts, 1)
            nc.gpsimd.affine_select(out=ident[:, :], in_=ident[:, :], compare_op=ALU.not_equal, fill=1.0,
                                    base=0, pattern=[[-1, P]], channel_multiplier=1).then_inc(consts, 1)
            nc.gpsimd.memset(eps[:, :], LN_EPS).then_inc(consts, 1)
            nc.gpsimd.iota(dist_i[:, :], pattern=[[-1, 256]], base=P, channel_multiplier=1).then_inc(consts, 1)
            pool.wait_ge(consts, 4)
            nc.gpsimd.tensor_copy(dist[:, :], dist_i[:, :]).then_inc(consts, 1)
            pool.wait_ge(consts, 5)
            nc.gpsimd.affine_select(out=dist[:, :], in_=dist[:, :], compare_op=ALU.is_ge, fill=MASKED,
                                    base=P, pattern=[[-1, 256]], channel_multiplier=1).then_inc(consts, 1)
            pool.wait_ge(consts, 6)
            nc.gpsimd.affine_select(out=dist[:, :], in_=dist[:, :], compare_op=ALU.is_ge, fill=MASKED,
                                    base=WINDOW - 1 - P, pattern=[[1, 256]], channel_multiplier=-1).then_inc(consts, 1)
            pool.wait_ge(consts, 7)
            pool.wait_ge(sinks_in, 16)

            def split_lo(third, off, h, wout=False):
                pool.wait_ge(hi_made, halves(third, off) + h + 1)
                whole = raw[:, off % 3, :]
                hi, lo = w_hi[:, half_slot(off, h), :].bitcast(F32), w_lo[:, half_slot(off, h), :]
                if wout:
                    nc.gpsimd.tensor_tensor(lo.rearrange("p (k n) -> p k n", n=512),
                                            whole.rearrange("p (k c n) -> p k c n", k=2, n=512)[:, :, h, :],
                                            hi.rearrange("p (k n) -> p k n", n=512), ALU.subtract).then_inc(lo_made, 1)
                else:
                    nc.gpsimd.tensor_tensor(lo, whole[:, h * HS:(h + 1) * HS], hi, ALU.subtract).then_inc(lo_made, 1)

            def biases(j, i):
                if i == 0:
                    pool.wait_ge(a_added, 32 * j + 1)
                    pool.sem_inc(waited_pool, 1)
                    nc.gpsimd.tensor_copy(sink_j[:, :], sink_all[:, bass.ds(GQA * j, GQA)]).then_inc(sink_set, 1)
                if i >= 2:
                    pool.wait_ge(s_read, 16 * j + 4 * (i - 1))
                    pool.sem_inc(waited_pool, 1)
                for h in range(2):
                    step = nc.gpsimd.tensor_scalar(bias[:, i % 2, h, :], dist[:, :], -SLOPE[2 * i + h], None, ALU.mult)
                step.then_inc(bias_set, 1)

            def attention(j, third, last):
                for i in range(TPJ):
                    split_lo(third, i + 2, 0, wout=(i == 3 and last))
                    biases(j, i)
                    split_lo(third, i + 2, 1, wout=(i == 3 and last))
                if not last:
                    pool.wait_ge(bias_set, TPJ * j + TPJ)
                    pool.sem_inc(waited_pool, 1)
                    nc.gpsimd.tensor_scalar(dist[:, :], dist[:, :], SLOPE_STEP, None, ALU.mult).then_inc(dist_set, 1)
                    pool.wait_ge(dist_set, j + 1)
                    for h in range(2):
                        split_lo(third, 6, h, wout=True)
                for r in range(4):
                    for h in range(2):
                        split_lo(third, (6 if last else 7) + r, h, wout=(r < 3))

            split_lo(0, 0, 0)
            pool.wait_ge(lo_made, 2)
            split_lo(0, 1, 0)
            split_lo(0, 1, 1)
            with pool.Fori(0, KVH - 1) as j:
                attention(j, 3 * j, False)
            attention(KVH - 1, 3 * (KVH - 1), True)

            for pair in range(2):
                for q in range(1, X1_GROUPS, 2):
                    pool.wait_ge(x1_hi_made, X1_GROUPS * pair + q + 1)
                    hi, lo = x1_group(xt_hi, pair, q), x1_group(xt_lo, pair, q)
                    full = x1t[:, q, :].rearrange("p (k n) -> p k n", n=PAIR)
                    nc.gpsimd.tensor_tensor(lo, full, hi.bitcast(F32), ALU.subtract).then_inc(x1_lo_pool, 1)
            pool.wait_ge(ln1_in, 32)
            for t in range(TT):
                pool.wait_ge(x1_tr, X1_GROUPS * (t // 2 + 1))
                nc.gpsimd.tensor_tensor(acc[:, t, :], acc[:, t, :], lng[:, :], ALU.mult).then_inc(gained, 1)
                pool.wait_ge(gained, t + 1)
                nc.gpsimd.tensor_tensor(acc[:, t, :], acc[:, t, :], lnb[:, :], ALU.add).then_inc(b_added, 1)
            pool.wait_ge(ln2_in, 32)
            for t in range(TT):
                cols = acc[:, t, DVE_COLS:D]
                pool.wait_ge(norm_cols, t + 1)
                nc.gpsimd.tensor_tensor(cols, cols, lng[:, DVE_COLS:D], ALU.mult).then_inc(gained, 1)
                pool.wait_ge(gained, TT + t + 1)
                nc.gpsimd.tensor_tensor(cols, cols, lnb[:, DVE_COLS:D], ALU.add).then_inc(ln_pool, 1)

        @block.scalar
        def _(act):
            def split_hi(third, off, h, first=False, arrived=False, kv=None, wout=False):
                if h == 0 and not arrived:
                    act.wait_ge(raw_in[off % 3], 16 * (third + off // 3 + 1))
                    if kv is not None:
                        act.wait_ge(rawv_in, 16 * (kv + 1))
                if not first:
                    act.wait_ge(w_used, halves(third, off) + h - 2)
                if wout:
                    nc.scalar.activation(w_hi[:, half_slot(off, h), :].rearrange("p (k n) -> p k n", n=512),
                                         raw[:, off % 3, :].rearrange("p (k c n) -> p k c n", k=2, n=512)[:, :, h, :],
                                         ACT.Copy).then_inc(hi_made, 1)
                else:
                    nc.scalar.activation(w_hi[:, half_slot(off, h), :], raw[:, off % 3, h * HS:(h + 1) * HS],
                                         ACT.Copy).then_inc(hi_made, 1)

            def xt_evac(t):
                for q in range(4):
                    e = 4 * t + q
                    act.wait_ge(xt_tr, e + 1)
                    nc.scalar.activation(xt_hi[:, 4 * q:4 * q + 4, t * P:(t + 1) * P],
                                         ps[:, XT_BANKS[e], :].rearrange("p (k n) -> p k n", n=P),
                                         ACT.Copy).then_inc(xt_hi_made, 1)

            def kv_evac(third, off, v_first):
                act.wait_ge(w_used, halves(third, off) + 2)
                if v_first:
                    nc.scalar.activation(vt[:, :], ps[64:128, KV_BANK, :], ACT.Copy).then_inc(vt_made, 1)
                nc.scalar.activation(k_hi[0:64, :], ps[0:64, KV_BANK, :], ACT.Copy)
                nc.scalar.activation(k_hi[64:128, :], ps[0:64, KV_BANK, :], ACT.Copy).then_inc(k_hi_made, 1)
                if not v_first:
                    nc.scalar.activation(vt[:, :], ps[64:128, KV_BANK, :], ACT.Copy).then_inc(vt_made, 1)

            def v_evac(m):
                act.wait_ge(v_tr, m + 1)
                nc.scalar.activation(v_st[:, :, 0:64], ps[:, PT_BANK, 0:256].rearrange("p (c d) -> p c d", d=64),
                                     ACT.Copy).then_inc(v_hi_made, 1)

            def q_evac(third, off, h, bank):
                act.wait_ge(w_used, halves(third, off) + 2)
                mine = slice(64 * h, 64 * h + 64)
                nc.scalar.activation(q_st[mine, h, :], ps[mine, bank, :], ACT.Copy, scale=SCALE).then_inc(q_hi_made, 1)

            def exps(a, i, h):
                act.wait_ge(negm_made, 2 * a + h + 1)
                nc.scalar.activation(esink[:, i % 2, h, :], negm[:, i % 2, h, :], ACT.Exp,
                                     bias=sink_j[:, 2 * i + h:2 * i + h + 1])
                for b in range(TT):
                    c0, own = block_cols(b)
                    c1 = own + 128
                    step = nc.scalar.activation(prob[:, i % 2, h, c0:c1], prob[:, i % 2, h, c0:c1], ACT.Exp,
                                                bias=negm[:, i % 2, h, b:b + 1],
                                                accum_out=rsum[:, i % 2, h, b:b + 1])
                step.then_inc(exp_made, 1)

            def pt_evac(b, y):
                n = 384 if y % 2 else 512
                if y >= 2:
                    act.wait_ge(pv_done, 4 * b + y - 1)
                act.wait_ge(pt_tr, 4 * b + y + 1)
                nc.scalar.activation(pt_hi[:, y % 2, 0:n], ps[:, PT_BANK, 0:n], ACT.Copy).then_inc(pt_hi_made, 1)

            def o_part(b, i, h):
                if i > 0 and h == 0:
                    act.wait_ge(o_lo_made, b)
                act.wait_ge(pv_done, 4 * b + 2 * h + 2)
                nc.scalar.activation(o_sum[64 * h:64 * h + 64, :], ps[64:128, PV_BANK, :],
                                     ACT.Copy).then_inc(o_part_made, 1)

            def o_evac(b, i):
                act.wait_ge(o_made, 2 * b + 2)
                nc.scalar.activation(ht_hi[:, i, :], o_sum[:, :], ACT.Copy).then_inc(o_hi_made, 1)

            def attention(j, third, last):
                a = 4 * j
                split_hi(third, 2, 0)
                split_hi(third, 2, 1)
                for i in range(1, 6):
                    nxt = i + 2
                    kv = j + 1 if (nxt == 5 and not last) else None
                    wout = nxt >= (5 if last else 6)
                    if i >= 3:
                        o_part(a + i - 3, i - 3, 1)
                    if i <= 4:
                        q_evac(third, i, 0, q_bank(i - 1, last))
                    elif not last:
                        kv_evac(third, 5, v_first=False)
                    if i in (3, 4):
                        o_evac(a + i - 3, i - 3)
                    if i <= 4:
                        q_evac(third, i, 1, q_bank(i - 1, last))
                    if i >= 2:
                        pt_evac(a + i - 2, 0)
                    if i == 5:
                        o_evac(a + 2, 2)
                    split_hi(third, nxt, 0, kv=kv, wout=wout)
                    if i >= 2:
                        pt_evac(a + i - 2, 1)
                    if i <= 4:
                        exps(a + i - 1, i - 1, 0)
                    if i >= 2:
                        o_part(a + i - 2, i - 2, 0)
                        pt_evac(a + i - 2, 2)
                    if i <= 4:
                        exps(a + i - 1, i - 1, 1)
                    if i >= 2:
                        pt_evac(a + i - 2, 3)
                    if i == 5:
                        o_part(a + 3, 3, 1)
                        o_evac(a + 3, 3)
                    split_hi(third, nxt, 1, wout=wout)
                if not last:
                    v_evac(j + 1)
                for r in range(2 if last else 1, 4):
                    for h in range(1 if last and r == 3 else 2):
                        split_hi(third, (6 if last else 7) + r, h, wout=(r < 3))

            def layer_norm_std(which, t):
                act.wait_ge(mean_made, TT * which + t + 1)
                nc.scalar.activation(std[:, t:t + 1], meanvar[:, t, 1:2], ACT.Sqrt,
                                     bias=eps[:, :]).then_inc(std_made, 1)

            def normalise(t):
                act.wait_ge(rstd_made, t + 1)
                act.wait_ge(shift_made, t + 1)
                for h in range(2):
                    cols = acc[:, t, h * D // 2:(h + 1) * D // 2]
                    nc.scalar.activation(cols, cols, ACT.Identity, scale=rstd[:, t:t + 1],
                                         bias=shift[:, t:t + 1]).then_inc(norm_act, 1)

            def x1_evac(pair, q):
                if pair:
                    act.wait_ge(x1_lo_pool if q % 2 else x1_lo_dve, q // 2 + 1)
                act.wait_ge(x1_tr, X1_GROUPS * pair + q + 1)
                bank = X1_BANKS[pair][q]
                for i in range(2):
                    k = 2 * q + i
                    step = nc.scalar.activation(x1t[:, q, i * PAIR:(i + 1) * PAIR],
                                                ps[:, bank, i * PAIR:(i + 1) * PAIR], ACT.Identity,
                                                scale=ln1_pk[:, k:k + 1], bias=ln1_pk[:, KD + k:KD + k + 1])
                step.then_inc(x1_made, 1)

            def layer_norm_1():
                layer_norm_std(0, 0)
                normalise(0)
                layer_norm_std(0, 1)
                split_hi(12, 0, 1)
                normalise(1)
                layer_norm_std(0, 2)
                for q in range(X1_GROUPS):
                    if q == 5:
                        layer_norm_std(0, 3)
                    x1_evac(0, q)
                split_hi(12, 1, 0)
                for q in range(X1_GROUPS):
                    x1_evac(1, q)

            def ffn_group(g, third, first=False, last=False):
                for c in range(GC):
                    for h in range(1 if first and c == 0 else 0, 2):
                        split_hi(third, 2 * c + 1, h)
                    act.wait_ge(w_used, halves(third, 2 * c) + 2)
                    nc.scalar.activation(sg[:, :], ps[:, 2 * c, :], ACT.Silu).then_inc(sg_made, 1)
                    for h in range(2):
                        split_hi(third, 2 * c + 2, h)
                    act.wait_ge(hm_made, 4 * g + c + 1)
                    nc.scalar.activation(ht_hi[:, c, :], hm[:, :], ACT.Copy).then_inc(h_hi_made, 1)
                for n in range(NN - 1 if last else NN):
                    for h in range(2):
                        split_hi(third, 2 * GC + n + 1, h)

            act.dma_start(sink_all[:, :], sinks[0, :].partition_broadcast(P)).then_inc(sinks_in, 16)
            act.dma_start(ln1_kp[0:KD, :], ln_g[0, 0, :].rearrange("(k p) -> k p", p=P)).then_inc(lnk_in, 16)
            act.dma_start(ln1_kp[KD:2 * KD, :], ln_b[0, 0, :].rearrange("(k p) -> k p", p=P)).then_inc(lnk_in, 16)
            xt_evac(0)
            act.wait_ge(kv0_in, 32)
            split_hi(0, 0, 0, first=True, arrived=True)
            xt_evac(1)
            act.wait_ge(raw_in[0], 16)
            act.wait_ge(rawv_in, 16)
            split_hi(0, 0, 1, first=True)
            for t in range(2, TT):
                xt_evac(t)
            split_hi(0, 1, 0, first=True)
            split_hi(0, 1, 1)
            kv_evac(0, 0, v_first=True)
            act.wait_ge(lnk_tr, 1)
            nc.scalar.activation(ln1_pk[:, :], ps[:, 7, 0:2 * KD], ACT.Copy).then_inc(lnk_made, 1)
            act.wait_ge(lnk_made, 1)
            act.wait_ge(consts, 3)
            v_evac(0)
            with act.Fori(0, KVH - 1) as j:
                attention(j, 3 * j, False)
            attention(KVH - 1, 3 * (KVH - 1), True)
            layer_norm_1()
            ffn_group(0, 12, first=True)
            with act.Fori(1, NG - 1) as g:
                ffn_group(g, 4 * g + 12)
            ffn_group(NG - 1, 4 * (NG - 1) + 12, last=True)
            for t in range(TT):
                layer_norm_std(1, t)
                act.wait_ge(rstd_made, TT + t + 1)
                act.wait_ge(shift_made, 2 + t + 1)
                cols = acc[:, t, DVE_COLS:D]
                nc.scalar.activation(cols, cols, ACT.Identity, scale=rstd[:, t:t + 1],
                                     bias=shift[:, t:t + 1]).then_inc(norm_cols, 1)

        @block.vector
        def _(dve):
            def split_lo(third, off, h):
                dve.wait_ge(hi_made, halves(third, off) + h + 1)
                nc.vector.tensor_tensor(w_lo[:, half_slot(off, h), :], raw[:, off % 3, h * HS:(h + 1) * HS],
                                        w_hi[:, half_slot(off, h), :].bitcast(F32), ALU.subtract).then_inc(lo_made, 1)

            def xt_evac(t):
                for q in range(4):
                    e = 4 * t + q
                    dve.wait_ge(xt_hi_made, e + 1)
                    nc.vector.tensor_tensor(xt_lo[:, 4 * q:4 * q + 4, t * P:(t + 1) * P],
                                            ps[:, XT_BANKS[e], :].rearrange("p (k n) -> p k n", n=P),
                                            xt_hi[:, 4 * q:4 * q + 4, t * P:(t + 1) * P].bitcast(F32),
                                            ALU.subtract).then_inc(xt_lo_made, 1)

            def kv_evac(m):
                dve.wait_ge(k_hi_made, m + 1)
                nc.vector.tensor_tensor(k_lo[0:64, :], ps[0:64, KV_BANK, :], k_hi[0:64, :].bitcast(F32), ALU.subtract)
                nc.vector.tensor_tensor(k_lo[64:128, :], ps[0:64, KV_BANK, :], k_hi[0:64, :].bitcast(F32),
                                        ALU.subtract).then_inc(k_lo_made, 1)

            def v_evac(m):
                dve.wait_ge(v_hi_made, m + 1)
                nc.vector.tensor_tensor(v_st[:, :, 64:128], ps[:, PT_BANK, 0:256].rearrange("p (c d) -> p c d", d=64),
                                        v_st[:, :, 0:64].bitcast(F32), ALU.subtract).then_inc(v_lo_made, 1)

            def q_evac(a, h, bank):
                top = slice(64 * h, 64 * h + 64)
                other = slice(64 - 64 * h, 128 - 64 * h)
                dve.wait_ge(q_hi_made, 2 * a + h + 1)
                nc.vector.scalar_tensor_tensor(out=q_st[other, h, :], in0=ps[top, bank, :], scalar=SCALE,
                                               in1=q_st[top, h, :].bitcast(F32), op0=ALU.mult,
                                               op1=ALU.subtract).then_inc(q_lo_made, 1)

            def scores(a, i, group):
                h, half = divmod(group, 2)
                if group == 0:
                    dve.wait_ge(bias_set, a + 1)
                dve.wait_ge(s_done, 4 * a + group + 1)
                dve.sem_inc(waited_dve, 1)
                at = 0
                for b in (2 * half, 2 * half + 1):
                    n = 128 if b == 0 else 256
                    c0 = block_cols(b)[0]
                    step = nc.vector.tensor_tensor_reduce(
                        out=prob[:, i % 2, h, c0:c0 + n], in0=ps[:, SCORE_BANK[group % 2], at:at + n],
                        in1=bias[:, i % 2, h, 256 - n:256], scale=1.0, scalar=-3.0e38, op0=ALU.add, op1=ALU.max,
                        accum_out=rmax[:, i % 2, h, b:b + 1])
                    at += n
                step.then_inc(s_read, 1)

            def neg_max(j, i, h):
                if h == 0 and i == 0:
                    dve.wait_ge(sink_set, j + 1)
                dve.wait_ge(s_read, 16 * j + 4 * i + 2 * h + 2)
                nc.vector.tensor_scalar(negm[:, i % 2, h, :], rmax[:, i % 2, h, :], sink_j[:, 2 * i + h:2 * i + h + 1],
                                        -1.0, ALU.max, ALU.mult).then_inc(negm_made, 1)

            def normalise(a, i, h):
                hd = 2 * a + h + 1
                dve.wait_ge(exp_made, hd)
                nc.vector.tensor_tensor(den[:, i % 2, h, :], rsum[:, i % 2, h, :], esink[:, i % 2, h, :],
                                        ALU.add).then_inc(den_made, 1)
                dve.wait_ge(den_made, hd)
                nc.vector.reciprocal(rden[:, i % 2, h, :], den[:, i % 2, h, :]).then_inc(rden_made, 1)
                dve.wait_ge(rden_made, hd)
                for b in range(TT):
                    c0 = block_cols(b)[0]
                    n = 128 if b == 0 else 256
                    step = nc.vector.tensor_scalar(prob[:, i % 2, h, c0:c0 + n], prob[:, i % 2, h, c0:c0 + n],
                                                   rden[:, i % 2, h, b:b + 1], None, ALU.mult)
                step.then_inc(p_made, 1)

            def pt_evac(b, y):
                n = 384 if y % 2 else 512
                dve.wait_ge(pt_hi_made, 4 * b + y + 1)
                nc.vector.tensor_tensor(pt_lo[:, y % 2, 0:n], ps[:, PT_BANK, 0:n], pt_hi[:, y % 2, 0:n].bitcast(F32),
                                        ALU.subtract).then_inc(pt_lo_made, 1)

            def o_add(b, h):
                dve.wait_ge(o_part_made, 2 * b + h + 1)
                o = o_sum[64 * h:64 * h + 64, :]
                nc.vector.tensor_tensor(o, o, ps[0:64, PV_BANK, :], ALU.add).then_inc(o_made, 1)

            def o_evac(b, i):
                dve.wait_ge(o_hi_made, b + 1)
                nc.vector.tensor_tensor(ht_lo[:, i, :], o_sum[:, :], ht_hi[:, i, :].bitcast(F32),
                                        ALU.subtract).then_inc(o_lo_made, 1)

            def add_wout(j, third, last, r, h, t):
                n = 2 * (r % 2) + h
                across = last and r == 3
                if t == TT - 1:
                    dve.wait_ge(w_used, halves(third, (5 if last else 6) + r) + h + 1)
                elif across:
                    dve.wait_ge(a_sum, 24 * j + 18 + 2 * t + h + 1)
                else:
                    dve.wait_ge(a_sum, 24 * j + 6 * r + 3 * h + t + 1)
                part = acc[:, t, n * 512:(n + 1) * 512]
                bank = 4 + t if across and h else t
                nc.vector.tensor_tensor(part, part, ps[:, bank, :], ALU.add).then_inc(a_added, 1)

            def part_stats(j, r, h, t):
                n = 2 * (r % 2) + h
                at = 2 * t + h if r == 3 else 4 * h + t
                dve.wait_ge(a_added, 4 + 32 * j + 8 * r + at + 1)
                nc.vector.bn_stats(stats[:, t, 6 * n:6 * n + 6], acc[:, t, n * 512:(n + 1) * 512]).then_inc(stat_made, 1)

            def attention(j, third, last):
                a = 4 * j
                for i in range(1, 6):
                    tile, b = i - 1, i - 2
                    r = i - 4 if last else i - 5
                    if i >= 3:
                        o_add(a + i - 3, 1)
                    if i <= 4:
                        q_evac(a + tile, 0, q_bank(tile, last))
                    elif not last:
                        kv_evac(j + 1)
                    if i in (3, 4):
                        o_evac(a + i - 3, i - 3)
                    if i <= 4:
                        q_evac(a + tile, 1, q_bank(tile, last))
                    if i >= 2:
                        pt_evac(a + b, 0)
                    if i == 5:
                        o_evac(a + 2, 2)
                    if r == 0:
                        dve.wait_ge(a_added, 32 * j + 4)
                    if i <= 4:
                        scores(a + tile, tile, 0)
                        scores(a + tile, tile, 1)
                        neg_max(j, tile, 0)
                    early = 2 if i == 5 and r >= 0 else 0
                    for t in range(early):
                        add_wout(j, third, last, r, 0, t)
                    if i >= 2:
                        pt_evac(a + b, 1)
                    if r >= 0:
                        for t in range(early, 3):
                            add_wout(j, third, last, r, 0, t)
                    if i <= 4:
                        scores(a + tile, tile, 2)
                        scores(a + tile, tile, 3)
                        neg_max(j, tile, 1)
                    if i <= 4 and r < 0:
                        normalise(a + tile, tile, 0)
                    if i >= 2:
                        o_add(a + b, 0)
                        pt_evac(a + b, 2)
                    if r >= 0:
                        add_wout(j, third, last, r, 0, 3)
                    if i <= 4 and r >= 0:
                        normalise(a + tile, tile, 0)
                    if r >= 0:
                        add_wout(j, third, last, r, 1, 0)
                    if i >= 2:
                        pt_evac(a + b, 3)
                    if r >= 0:
                        add_wout(j, third, last, r, 1, 1)
                    if r >= 0:
                        add_wout(j, third, last, r, 1, 2)
                    if i <= 4:
                        normalise(a + tile, tile, 1)
                    if i == 5:
                        o_add(a + 3, 1)
                    if r >= 0:
                        add_wout(j, third, last, r, 1, 3)
                o_evac(a + 3, 3)
                if not last:
                    v_evac(j + 1)
                for r in range(2 if last else 1, 4):
                    if last and r == 3:
                        for t in range(TT):
                            add_wout(j, third, last, r, 0, t)
                            if t > 0:
                                scales(0, t - 1)
                            add_wout(j, third, last, r, 1, t)
                            if t < TT - 1:
                                part_stats(j, r, 0, t)
                                part_stats(j, r, 1, t)
                                moments(t)
                    else:
                        for h in range(2):
                            for t in range(TT):
                                add_wout(j, third, last, r, h, t)
                                if last and (h, t) > (0, 0):
                                    part_stats(j, r, h if t else 0, (t - 1) % TT)
                        if last:
                            part_stats(j, r, 1, TT - 1)

            def add_wdown_tile(g, n, third, off, t, first, last):
                if t < TT - 1:
                    dve.wait_ge(b_sum, 12 * g + 3 * n + t + 1)
                else:
                    dve.wait_ge(w_used, halves(third, off) + 2)
                part = acc[:, t, n * 512:(n + 1) * 512]
                if first:
                    nc.vector.scalar_tensor_tensor(out=part, in0=part, scalar=ALPHA,
                                                   in1=ps[:, B_BANKS[n % 2][t], :], op0=ALU.mult,
                                                   op1=ALU.add).then_inc(b_added, 1)
                else:
                    nc.vector.tensor_tensor(part, part, ps[:, B_BANKS[n % 2][t], :], ALU.add).then_inc(b_added, 1)
                if last:
                    dve.wait_ge(b_added, 4 + 16 * g + 4 * n + t + 1)
                    nc.vector.bn_stats(stats[:, t, 6 * n:6 * n + 6], part).then_inc(stat_made, 1)

            def scale_residual():
                for t in range(TT):
                    nc.vector.tensor_scalar(acc[:, t, :], acc[:, t, :], ALPHA, None, ALU.mult).then_inc(a_added, 1)

            def moments(t):
                dve.wait_ge(stat_made, 8 + 2 * t + 2)
                nc.vector.bn_aggr(meanvar[:, t, :], stats[:, t, :]).then_inc(mean_made, 1)

            def scales(which, t):
                n = TT * which + t + 1
                dve.wait_ge(std_made, n)
                nc.vector.reciprocal(rstd[:, t:t + 1], std[:, t:t + 1]).then_inc(rstd_made, 1)
                dve.wait_ge(mean_made, n)
                dve.wait_ge(rstd_made, n)
                if which == 1 or t < 2:
                    nc.vector.scalar_tensor_tensor(out=shift[:, t:t + 1], in0=meanvar[:, t, 0:1], scalar=-1.0,
                                                   in1=rstd[:, t:t + 1], op0=ALU.mult,
                                                   op1=ALU.mult).then_inc(shift_made, 1)

            def normalise_x(t):
                dve.wait_ge(rstd_made, t + 1)
                nc.vector.tensor_scalar(acc[:, t, :], acc[:, t, :], meanvar[:, t, 0:1], rstd[:, t:t + 1],
                                        ALU.subtract, ALU.mult).then_inc(norm_dve, 1)

            def x1_split(pair, q):
                hi, lo = x1_group(xt_hi, pair, q), x1_group(xt_lo, pair, q)
                full = x1t[:, q, :].rearrange("p (k n) -> p k n", n=PAIR)
                n = X1_GROUPS * pair + q + 1
                dve.wait_ge(x1_made, n)
                nc.vector.tensor_copy(hi, full).then_inc(x1_hi_made, 1)
                if q % 2 == 0:
                    dve.wait_ge(x1_hi_made, n)
                    nc.vector.tensor_tensor(lo, full, hi.bitcast(F32), ALU.subtract).then_inc(x1_lo_dve, 1)

            def layer_norm_2(t):
                if t == 0:
                    dve.wait_ge(ln2_in, 32)
                dve.wait_ge(mean_made, TT + t + 1)
                cols = acc[:, t, 0:DVE_COLS]
                nc.vector.scalar_tensor_tensor(out=cols, in0=cols, scalar=meanvar[:, t, 0:1], in1=lng[:, 0:DVE_COLS],
                                               op0=ALU.subtract, op1=ALU.mult).then_inc(centered, 1)

            def layer_norm_2_end(t):
                dve.wait_ge(rstd_made, TT + t + 1)
                dve.wait_ge(centered, t + 1)
                for lo, hi in PIECES if t == TT - 1 else [(0, DVE_COLS)]:
                    cols = acc[:, t, lo:hi]
                    nc.vector.scalar_tensor_tensor(out=cols, in0=cols, scalar=rstd[:, t:t + 1], in1=lnb[:, lo:hi],
                                                   op0=ALU.mult, op1=ALU.add).then_inc(ln_made, 1)

            def last_wdown_unit(third, off):
                for t in range(TT):
                    add_wdown_tile(NG - 1, NN - 1, third, off, t, False, True)
                    dve.wait_ge(stat_made, 16 + 12 + t + 1)
                    nc.vector.bn_aggr(meanvar[:, t, :], stats[:, t, :]).then_inc(mean_made, 1)
                    if t > 0:
                        layer_norm_2(t - 1)
                    scales(1, t)
                    if t > 0:
                        layer_norm_2_end(t - 1)
                layer_norm_2(TT - 1)
                layer_norm_2_end(TT - 1)

            def ffn_group(g, third, first=False, last=False):
                for c in range(GC):
                    for u in (2 * c + 1, 2 * c + 2):
                        for h in range(1 if first and u == 1 else 0, 2):
                            split_lo(third, u, h)
                    dve.wait_ge(w_used, halves(third, 2 * c + 1) + 2)
                    dve.wait_ge(sg_made, 4 * g + c + 1)
                    nc.vector.tensor_tensor(hm[:, :], sg[:, :], ps[:, 2 * c + 1, :], ALU.mult).then_inc(hm_made, 1)
                    dve.wait_ge(h_hi_made, 4 * g + c + 1)
                    nc.vector.tensor_tensor(ht_lo[:, c, :], hm[:, :], ht_hi[:, c, :].bitcast(F32),
                                            ALU.subtract).then_inc(h_lo_made, 1)
                dve.wait_ge(b_added, 16 * g + 4)
                for n in range(NN):
                    if not (last and n == NN - 1):
                        for h in range(2):
                            split_lo(third, 2 * GC + n + 1, h)
                    if last and n == NN - 1:
                        last_wdown_unit(third, 2 * GC + n)
                    else:
                        for t in range(TT):
                            add_wdown_tile(g, n, third, 2 * GC + n, t, first, last)

            xt_evac(0)
            xt_evac(1)
            dve.wait_ge(lo_made, 1)
            split_lo(0, 0, 1)
            xt_evac(2)
            xt_evac(3)
            scale_residual()
            kv_evac(0)
            v_evac(0)
            with dve.Fori(0, KVH - 1) as j:
                attention(j, 3 * j, False)
            attention(KVH - 1, 3 * (KVH - 1), True)
            for q in range(X1_GROUPS):
                if q == 2:
                    part_stats(KVH - 1, 3, 0, 3)
                    part_stats(KVH - 1, 3, 1, 3)
                    moments(3)
                if q == 6:
                    scales(0, 3)
                if q in (4, 6):
                    normalise_x(q // 2)
                x1_split(0, q)
            dve.wait_ge(lo_made, halves(12, 0) + 2)
            split_lo(12, 1, 0)
            for q in range(X1_GROUPS):
                x1_split(1, q)
            ffn_group(0, 12, first=True)
            with dve.Fori(1, NG - 1) as g:
                ffn_group(g, 4 * g + 12)
            ffn_group(NG - 1, 4 * (NG - 1) + 12, last=True)

        @block.tensor
        def _(pe):
            def transpose_rows(t):
                pe.wait_ge(x_in[t], 16)
                for q in range(4):
                    e = 4 * t + q
                    bank = XT_BANKS[e]
                    if e >= 8:
                        pe.wait_ge(xt_lo_made, e - 1 - XT_BANKS[:e][::-1].index(bank) + 1)
                    for k in range(4):
                        kk = 4 * q + k
                        step = nc.tensor.transpose(ps[:, bank, k * P:(k + 1) * P],
                                                   acc[:, t, kk * P:(kk + 1) * P], ident[:, :])
                    step.then_inc(xt_tr, 1)

            def transpose_x1(pair, steps):
                for half, i in steps:
                    groups = range(4 * half, 4 * half + 4)
                    t = 2 * pair + i
                    if pair == 0:
                        pe.wait_ge(norm_act, 2 * i + half + 1)
                    elif half == 0:
                        pe.wait_ge(norm_dve, i + 1)
                    for q in groups:
                        bank = X1_BANKS[pair][q]
                        if i == 0 and pair == 0:
                            pe.wait_ge(a_added, 4 + 32 * (KVH - 1) + 24 + 2 * (bank % 4) + bank // 4 + 1)
                        elif i == 0:
                            pe.wait_ge(x1_made, q + 3)
                        for c in range(2):
                            k = 2 * q + c
                            at = c * PAIR + i * P
                            step = nc.tensor.transpose(ps[:, bank, at:at + P], acc[:, t, k * P:(k + 1) * P],
                                                       ident[:, :])
                        if i == 1:
                            step.then_inc(x1_tr, 1)

            def column_step(third, off, k, bank, pair=None, done=True, group=None):
                start, stop = group or (k == 0, k == KD - 1)
                mixed = group is not None
                tok = slice(0, S) if pair is None else slice(pair * PAIR, (pair + 1) * PAIR)
                h, kk = divmod(k, 8)
                s = half_slot(off, h)
                if kk == 0:
                    pe.wait_ge(lo_made, halves(third, off) + h + 1)
                hi = w_hi[:, s, kk * P:(kk + 1) * P]
                lo = w_lo[:, s, kk * P:(kk + 1) * P]
                nc.tensor.matmul(ps[:, bank, tok], hi, xt_lo[:, k, tok], start=start, stop=False,
                                 skip_group_check=mixed)
                nc.tensor.matmul(ps[:, bank, tok], hi, xt_hi[:, k, tok], start=False, stop=False,
                                 skip_group_check=mixed)
                step = nc.tensor.matmul(ps[:, bank, tok], lo, xt_hi[:, k, tok], start=False, stop=stop,
                                        skip_group_check=mixed)
                if kk == 7 and done:
                    step.then_inc(w_used, 1)

            def row_products(s, wk, kk, t, bank, first, last):
                hi = w_hi[:, s, wk * 512:(wk + 1) * 512]
                lo = w_lo[:, s, wk * 512:(wk + 1) * 512]
                tok = slice(t * P, (t + 1) * P)
                nc.tensor.matmul(ps[:, bank, :], ht_hi[:, kk, tok], lo, start=first, stop=False)
                nc.tensor.matmul(ps[:, bank, :], ht_hi[:, kk, tok], hi, start=False, stop=False)
                return nc.tensor.matmul(ps[:, bank, :], ht_lo[:, kk, tok], hi, start=False, stop=last)

            def wdown_step(g, third, n, kk, t):
                off = 2 * GC + n
                h, wk = divmod(kk, 2)
                if wk == 0 and t == 0:
                    pe.wait_ge(lo_made, halves(third, off) + h + 1)
                if kk == 0 and n >= 2:
                    pe.wait_ge(b_added, 16 * g + 4 + 4 * (n - 2) + t + 1)
                step = row_products(half_slot(off, h), wk, kk, t, B_BANKS[n % 2][t], kk == 0, kk == 3)
                if wk == 1 and t == TT - 1:
                    step.then_inc(w_used, 1)
                elif kk == 3:
                    step.then_inc(b_sum, 1)

            def wout_step(j, third, last, r, h, kk, t):
                off = (5 if last else 6) + r
                across = last and r == 3
                bank = 4 + t if across and h else t
                if kk == 0 and t == 0:
                    pe.wait_ge(lo_made, halves(third, off) + h + 1)
                if kk == 0 and across and h == 0:
                    pe.wait_ge(a_added, 32 * j + 8 * r + t + 1)
                elif kk == 0 and not across and (r, h) != (0, 0):
                    pe.wait_ge(a_added, 32 * j + 8 * r + 4 * h + t + 1)
                step = row_products(half_slot(off, h), kk, 2 * (r // 2) + kk, t, bank, kk == 0, kk == 1)
                if kk == 1 and t == TT - 1:
                    step.then_inc(w_used, 1)
                elif kk == 1:
                    step.then_inc(a_sum, 1)

            def scores(a, i, j, group):
                h, half = divmod(group, 2)
                bank = SCORE_BANK[group % 2]
                if i == 0 and group == 0:
                    pe.wait_ge(k_lo_made, j + 1)
                if i > 0 or group >= 2:
                    pe.wait_ge(s_read, 4 * a + group - 1)
                if half == 0:
                    pe.wait_ge(q_lo_made, 2 * a + h + 1)
                at = 0
                for b in (2 * half, 2 * half + 1):
                    n = 128 if b == 0 else 256
                    keys = slice((b + 1) * P - n, (b + 1) * P)
                    q = q_st[:, h, b * P:(b + 1) * P]
                    nc.tensor.matmul(ps[:, bank, at:at + n], q, k_lo[:, keys], start=True, stop=False)
                    step = nc.tensor.matmul(ps[:, bank, at:at + n], q, k_hi[:, keys], start=False, stop=True)
                    at += n
                step.then_inc(s_done, 1)

            def transpose_p(b, i, j, y):
                h, half = divmod(y, 2)
                if half == 0:
                    pe.wait_ge(p_made, 2 * b + h + 1)
                if i > 0 or y > 0:
                    pe.wait_ge(pt_lo_made, 4 * b + y)
                else:
                    pe.wait_ge(v_lo_made, j + 1)
                at = 0
                for c in (2 * half, 2 * half + 1):
                    own = block_cols(c)[1]
                    step = nc.tensor.transpose(ps[:, PT_BANK, at:at + P], prob[:, i % 2, h, own:own + P], ident[:, :])
                    at += P
                    if c < TT - 1:
                        prev = block_cols(c + 1)[0]
                        step = nc.tensor.transpose(ps[:, PT_BANK, at:at + P], prob[:, i % 2, h, prev:prev + P],
                                                   ident[:, :])
                        at += P
                step.then_inc(pt_tr, 1)

            def p_times_v(b, i, j, y):
                h, half = divmod(y, 2)
                if y == 0 and i > 0:
                    pe.wait_ge(o_made, 2 * b)
                if y == 2:
                    pe.wait_ge(o_made, 2 * b + 1)
                pe.wait_ge(pt_lo_made, 4 * b + y + 1)
                at = 0
                for c in (2 * half, 2 * half + 1):
                    n = 256 if c < TT - 1 else 128
                    o = ps[:, PV_BANK, c * P:c * P + n]
                    nc.tensor.matmul(o, v_st[:, c, :], pt_lo[:, y % 2, at:at + n], start=(c == 0), stop=False,
                                     skip_group_check=True)
                    step = nc.tensor.matmul(o, v_st[:, c, :], pt_hi[:, y % 2, at:at + n], start=False,
                                            stop=(c == TT - 1), skip_group_check=True)
                    at += n
                step.then_inc(pv_done, 1)

            def transpose_v(m, groups):
                pe.wait_ge(vt_made, m + 1)
                if groups is not None:
                    pe.wait_ge(pt_lo_made, groups)
                pe.sem_inc(waited_pe, 1)
                for c in range(TT):
                    step = nc.tensor.transpose(ps[:, PT_BANK, 64 * c:64 * c + 64], vt[:, c * P:(c + 1) * P],
                                               ident[0:64, 0:64])
                step.then_inc(v_tr, 1)

            def beside(k, i, j):
                tile, b = i - 1, i - 2
                if 0 <= tile < TPJ and k in (3, 4, 6, 7):
                    scores(4 * j + tile, tile, j, (3, 4, 6, 7).index(k))
                if b >= 0:
                    at = (1, 5, 9, 12, 15) if b < 3 else (0, 4, 8, 11, 14)
                    if k in at[1:]:
                        p_times_v(4 * j + b, b, j, at.index(k) - 1)
                    if k in at[:4]:
                        transpose_p(4 * j + b, b, j, at.index(k))

            def attention(j, third, last):
                pe.wait_ge(a_added, 32 * j + 1)
                for k in range(KD):
                    column_step(third, 1, k, q_bank(0, last))
                pe.wait_ge(a_added, 32 * j + 4)
                for i in range(1, 4 if last else 5):
                    for k in range(KD):
                        column_step(third, 1 + i, k, KV_BANK if i == 4 else q_bank(i, last))
                        beside(k, i, j)
                for r in range(4):
                    i = r + (4 if last else 5)
                    if r == 2:
                        pe.wait_ge(o_lo_made, 4 * j + 3)
                    if last and r == 3:
                        pe.wait_ge(lo_made, halves(third, 5 + r) + 2)
                        for t in range(TT):
                            for h in range(2):
                                for kk in range(2):
                                    wout_step(j, third, last, r, h, kk, t)
                        continue
                    for h in range(2):
                        order = FIRST_HALF if (r, h) in ((0, 0), (2, 0)) else TILE_ORDER
                        for s, (kk, t) in enumerate(order):
                            if (r, h) == (2, 0) and (kk, t) == (1, 0):
                                pe.wait_ge(o_lo_made, 4 * j + 4)
                            if (r, h) == (0, 0) and (kk, t) == (0, 0):
                                pe.wait_ge(o_lo_made, 4 * j + 1)
                            if (r, h) == (0, 0) and (kk, t) == (1, 0):
                                pe.wait_ge(o_lo_made, 4 * j + 2)
                            if (r, h) == (0, 0) and (kk, t) == (0, 3):
                                if last:
                                    pe.wait_ge(q_lo_made, 8 * j + 8)
                                else:
                                    pe.wait_ge(k_lo_made, j + 2)
                            wout_step(j, third, last, r, h, kk, t)
                            if i <= 5:
                                beside(8 * h + s, i, j)
                            if not last and r == 1 and 8 * h + s == 2:
                                transpose_v(j + 1, 16 * j + 16)

            def first_ffn_units():
                def x1_ready(pair, k):
                    if k % 4 == 0:
                        pe.wait_ge(x1_lo_dve, X1_GROUPS // 2 * pair + k // 4 + 1)
                    elif k % 4 == 2:
                        pe.wait_ge(x1_lo_pool, X1_GROUPS // 2 * pair + k // 4 + 1)

                transpose_x1(0, [(0, 0), (0, 1), (1, 0), (1, 1)])
                for k in range(KD):
                    x1_ready(0, k)
                    column_step(12, 0, k, 0, pair=0, done=False)
                    if k == 11:
                        transpose_x1(1, [(0, 0)])
                transpose_x1(1, [(0, 1), (1, 0), (1, 1)])
                for k in range(KD // 2):
                    column_step(12, 1, k, 1, pair=0, done=False, group=(k == 0, False))
                for k in range(KD):
                    x1_ready(1, k)
                    column_step(12, 0, k, 0, pair=1)
                for k in range(KD // 2):
                    column_step(12, 1, k, 1, pair=1, group=(False, False))
                for k in range(KD // 2, KD):
                    for pair in range(2):
                        column_step(12, 1, k, 1, pair=pair, done=(pair == 1), group=(False, k == KD - 1 and pair == 1))

            def ffn_group(g, third, first=False, last=False):
                if first:
                    first_ffn_units()
                for c in range(1 if first else 0, GC):
                    for up in range(2):
                        if up == 0 and c == 0:
                            pe.wait_ge(b_added, 16 * g + 1)
                        if up == 0 and c == 2 and not first:
                            pe.wait_ge(b_added, 16 * g + 4)
                        for k in range(KD):
                            column_step(third, 2 * c + up, k, 2 * c + up)
                for n in range(NN):
                    if last and n == NN - 1:
                        for t in range(TT):
                            for kk in range(4):
                                wdown_step(g, third, n, kk, t)
                        continue
                    for kk in range(4):
                        if n == 0:
                            pe.wait_ge(h_lo_made, 4 * g + max(kk + 1, 2))
                        for t in range(TT):
                            wdown_step(g, third, n, kk, t)

            pe.wait_ge(consts, 2)
            transpose_rows(0)
            for _ in range(FILL):
                nc.tensor.transpose(ps[:, 7, 0:P], ident[:, :], ident[:, :])
            transpose_rows(1)
            for pair in range(2):
                for k in range(KD):
                    if k % 4 == 0:
                        pe.wait_ge(xt_lo_made, 8 * pair + 4 + k // 4 + 1)
                    column_step(0, 0, k, KV_BANK, pair=pair, done=(pair == 1))
                    if pair == 0 and k in (11, 13):
                        transpose_rows(2 if k == 11 else 3)
            pe.wait_ge(lnk_in, 32)
            nc.tensor.transpose(ps[:, 7, 0:2 * KD], ln1_kp[:, :], ident[0:2 * KD, 0:2 * KD]).then_inc(lnk_tr, 1)
            transpose_v(0, None)
            with pe.Fori(0, KVH - 1) as j:
                attention(j, 3 * j, False)
            attention(KVH - 1, 3 * (KVH - 1), True)
            ffn_group(0, 12, first=True)
            with pe.Fori(1, NG - 1) as g:
                ffn_group(g, 4 * g + 12)
            ffn_group(NG - 1, 4 * (NG - 1) + 12, last=True)


_INS = ["x", "a_w_in", "a_sinks", "a_w_out", "ln_g", "ln_b", "ffn_w_gate_up", "ffn_w_down"]


def kernel(**inputs):
    import numpy as _np
    import concourse.bacc as _bacc
    from concourse import mybir as _mybir
    from concourse.bass_utils import run_bass_kernel_spmd as _run

    nc = _bacc.Bacc("TRN2", target_bir_lowering=False, num_devices=1)
    arrays, args = {}, []
    for name in _INS:
        a = _np.ascontiguousarray(inputs[name])
        arrays[f"in_{name}"] = a
        args.append(nc.dram_tensor(f"in_{name}", a.shape, _mybir.dt.from_np(a.dtype), kind="ExternalInput").ap())
    shape = inputs["x"].shape
    result = nc.dram_tensor("out_rows", shape, _mybir.dt.float32, kind="ExternalOutput").ap()
    trunk_layer(nc, *args, result)
    r = _run(nc, [arrays], core_ids=[0])
    return r.results[0]["out_rows"]
```
